# Optimizing a Trainium2 kernel written in Bass

```python
import jax, jax.numpy as jnp
from jax import lax
import numpy as np

D_MODEL = 1024
BATCH = 1
SEQ = 256
DEPTH = 2

N_A_LAYERS = DEPTH // 2
N_B_LAYERS = DEPTH - N_A_LAYERS
CONV_WIDTH = 3
SB_HEADS = 16
SB_HEAD_DIM = D_MODEL // SB_HEADS
Q_BLOCK = 128
PEER_HEADS = 8
PEER_N_KEYS = 128
PEER_N_EXPERTS = PEER_N_KEYS * PEER_N_KEYS
PEER_KEY_DIM = 128
PEER_QUERY_DIM = 2 * PEER_KEY_DIM
PEER_TOPK = 16
TOKEN_CHUNK = 128
RMS_EPS = 1e-6

kernel_name = "yoco_shortconv_stickbreaking_peer"

def rmsnorm(x, g):
    xf = x.astype(jnp.float32)
    y = xf * lax.rsqrt(jnp.mean(xf * xf, axis=-1, keepdims=True) + RMS_EPS)
    return (y * g.astype(jnp.float32)).astype(x.dtype)

def short_conv_mixer(xn, w_in, conv_k, w_out):
    L = xn.shape[1]
    b_gate, c_gate, h = jnp.split(xn @ w_in, 3, axis=-1)
    u = c_gate * h
    up = jnp.pad(u, ((0, 0), (CONV_WIDTH - 1, 0), (0, 0)))
    conv = up[:, 0:L] * conv_k[0]
    for i in range(1, CONV_WIDTH):
        conv = conv + up[:, i:i + L] * conv_k[i]
    return (b_gate * conv) @ w_out

def stick_breaking_attention(q, k, v):
    B, S, H, Dh = q.shape
    nb = S // Q_BLOCK
    scale = Dh ** -0.5
    q_blocks = q.reshape(B, nb, Q_BLOCK, H, Dh).transpose(1, 0, 3, 2, 4)
    k_pos = jnp.arange(S)

    def one_block(args):
        q_blk, blk = args
        z = jnp.einsum('bhqd,bhkd->bhqk', q_blk, k).astype(jnp.float32) * scale
        q_pos = blk * Q_BLOCK + jnp.arange(Q_BLOCK)
        causal = k_pos[None, :] < q_pos[:, None]
        log_not = jnp.where(causal, jax.nn.log_sigmoid(-z), 0.0)
        after = lax.cumsum(log_not, axis=3, reverse=True) - log_not
        w = jnp.where(causal, jnp.exp(jax.nn.log_sigmoid(z) + after), 0.0)
        return jnp.einsum('bhqk,bhkd->bhqd', w.astype(v.dtype), v)

    out = lax.map(one_block, (q_blocks, jnp.arange(nb)))
    return out.transpose(1, 0, 3, 2, 4).reshape(B, S, H * Dh)

def peer_ffn(xn, w_query, subkeys, u_tbl, v_tbl):
    B, S, D = xn.shape
    tok = xn.reshape(-1, TOKEN_CHUNK, D)

    def one_chunk(xc):
        C = xc.shape[0]
        q = (xc @ w_query).reshape(C, PEER_HEADS, 2, PEER_KEY_DIM)
        s = jnp.einsum('chpd,hpnd->chpn', q, subkeys).astype(jnp.float32)
        s1, i1 = lax.top_k(s[:, :, 0], PEER_TOPK)
        s2, i2 = lax.top_k(s[:, :, 1], PEER_TOPK)
        cand = (s1[..., :, None] + s2[..., None, :]).reshape(C, PEER_HEADS, PEER_TOPK * PEER_TOPK)
        top_s, top_c = lax.top_k(cand, PEER_TOPK)
        idx = (jnp.take_along_axis(i1, top_c // PEER_TOPK, axis=-1) * PEER_N_KEYS
               + jnp.take_along_axis(i2, top_c % PEER_TOPK, axis=-1))
        gate = jax.nn.softmax(top_s, axis=-1)
        act = jax.nn.gelu(jnp.einsum('chkd,cd->chk', u_tbl[idx], xc).astype(jnp.float32), approximate=False)
        coef = (gate * act).astype(xc.dtype)
        return jnp.einsum('chk,chkd->cd', coef, v_tbl[idx])

    return lax.map(one_chunk, tok).reshape(B, S, D)

def setup_inputs(seed: int = 0) -> dict:
    key = jax.random.key(seed)
    ks = jax.random.split(key, 16)
    D = D_MODEL
    f32 = jnp.float32
    nrm = lambda k, shape, s: jax.random.normal(k, shape, f32) * s
    return {
        "x": nrm(ks[0], (BATCH, SEQ, D), 1.0),
        "norm_mix": 1.0 + nrm(ks[1], (DEPTH, D), 0.02),
        "norm_ffn": 1.0 + nrm(ks[2], (DEPTH, D), 0.02),
        "conv_w_in": nrm(ks[3], (N_A_LAYERS, D, 3 * D), D ** -0.5),
        "conv_kernel": nrm(ks[4], (N_A_LAYERS, CONV_WIDTH, D), CONV_WIDTH ** -0.5),
        "conv_w_out": nrm(ks[5], (N_A_LAYERS, D, D), D ** -0.5),
        "norm_kv": 1.0 + nrm(ks[6], (D,), 0.02),
        "w_kv": nrm(ks[7], (D, 2 * SB_HEADS * SB_HEAD_DIM), D ** -0.5),
        "attn_w_q": nrm(ks[8], (N_B_LAYERS, D, SB_HEADS * SB_HEAD_DIM), D ** -0.5),
        "attn_w_o": nrm(ks[9], (N_B_LAYERS, SB_HEADS * SB_HEAD_DIM, D), D ** -0.5),
        "peer_w_query": nrm(ks[10], (DEPTH, D, PEER_HEADS * PEER_QUERY_DIM), D ** -0.5),
        "peer_subkeys": nrm(ks[11], (DEPTH, PEER_HEADS, 2, PEER_N_KEYS, PEER_KEY_DIM), PEER_KEY_DIM ** -0.5),
        "peer_u": nrm(ks[12], (DEPTH, PEER_N_EXPERTS, D), D ** -0.5),
        "peer_v": nrm(ks[13], (DEPTH, PEER_N_EXPERTS, D), PEER_HEADS ** -0.5),
        "norm_final": 1.0 + nrm(ks[14], (D,), 0.02),
    }

def reference(x, norm_mix, norm_ffn, conv_w_in, conv_kernel, conv_w_out, norm_kv, w_kv,
              attn_w_q, attn_w_o, peer_w_query, peer_subkeys, peer_u, peer_v, norm_final):
    B, S, D = x.shape
    h = x
    k_shared = None
    v_shared = None
    for layer in range(DEPTH):
        xn = rmsnorm(h, norm_mix[layer])
        if layer < N_A_LAYERS:
            h = h + short_conv_mixer(xn, conv_w_in[layer], conv_kernel[layer], conv_w_out[layer])
        else:
            j = layer - N_A_LAYERS
            q = (xn @ attn_w_q[j]).reshape(B, S, SB_HEADS, SB_HEAD_DIM)
            h = h + stick_breaking_attention(q, k_shared, v_shared) @ attn_w_o[j]
        h = h + peer_ffn(rmsnorm(h, norm_ffn[layer]), peer_w_query[layer], peer_subkeys[layer],
                         peer_u[layer], peer_v[layer])
        if layer == N_A_LAYERS - 1:
            k_flat, v_flat = jnp.split(rmsnorm(h, norm_kv) @ w_kv, 2, axis=-1)
            k_shared = k_flat.reshape(B, S, SB_HEADS, SB_HEAD_DIM).transpose(0, 2, 1, 3)
            v_shared = v_flat.reshape(B, S, SB_HEADS, SB_HEAD_DIM).transpose(0, 2, 1, 3)
    return rmsnorm(h, norm_final)


_drawn_inputs = setup_inputs


def setup_inputs(seed=0):
    import zlib

    import numpy as np

    out = dict(_drawn_inputs(seed))
    spreads = {}
    factors = {'norm_kv': 3.89, 'norm_final': 2.877}
    for name, (base, spread) in spreads.items():
        noise = np.random.default_rng([zlib.crc32(name.encode()), seed]).standard_normal(out[name].shape)
        drawn = base * np.exp(spread * noise) if base else spread * noise
        out[name] = __import__('jax').numpy.asarray(drawn.astype(out[name].dtype))
    for name, factor in factors.items():
        out[name] = (out[name] * factor).astype(out[name].dtype)
    return out
```

```python
from contextlib import ExitStack

import concourse.bass as bass
from concourse import mybir

F32 = mybir.dt.float32
U32 = mybir.dt.uint32
ALU = mybir.AluOpType
ACT = mybir.ActivationFunctionType
AX_X = mybir.AxisListType.X

P = 128
EPS = 1e-6
FOUND = -3.0e38
MASKED = -1.0e4
COLS = 256
W_RING = 4
U_SLOTS = 8
V_SLOTS = 16
GROUP = 8


def trunk(nc, x, norm_mix, norm_ffn, conv_w_in, conv_kernel, conv_w_out, norm_kv, w_kv,
          attn_w_q, attn_w_o, peer_w_query, peer_subkeys, peer_u, peer_v, norm_final, out):
    _, T, D = x.shape
    LAYERS, HEADS, _, KEYS, KD = peer_subkeys.shape
    EXPERTS = peer_u.shape[1]
    TAPS = conv_kernel.shape[1]
    CH = T // P
    KT = D // P
    TOPK = 16
    DH = 64
    PAIRS = D // (2 * DH)
    NH = CH * HEADS
    GROUPS = TOPK // GROUP
    assert (CH, KEYS, KD, COLS) == (2, P, P, 2 * P) and GROUPS == 2 and D == PAIRS * P and KT == PAIRS
    assert U_SLOTS == GROUP and V_SLOTS == TOPK and TAPS == 3 and LAYERS == 2

    blocks = []
    for j in range(D // COLS):
        blocks += [(conv_w_in[0], part * D + j * COLS, by) for part, by in ((2, "act"), (1, "dve"), (0, "dve"))]
    CONV = 0
    W_OUT = len(blocks)
    blocks += [(conv_w_out[0], j * COLS, "dve") for j in range(D // COLS)]
    QUERY = [len(blocks), 0]
    blocks += [(peer_w_query[0], j * COLS, "act") for j in range(HEADS)]
    W_K = len(blocks)
    blocks += [(w_kv, j * COLS, "act") for j in range(D // COLS)]
    W_V = len(blocks)
    blocks += [(w_kv, D + j * COLS, "act") for j in range(D // COLS)]
    W_Q = len(blocks)
    blocks += [(attn_w_q[0], j * COLS, "act") for j in range(D // COLS)]
    W_O = len(blocks)
    blocks += [(attn_w_o[0], j * COLS, "dve") for j in range(D // COLS)]
    QUERY[1] = len(blocks)
    blocks += [(peer_w_query[1], j * COLS, "act") for j in range(HEADS)]
    readers = [b[2] for b in blocks]

    fills = []

    def reserve(n, by):
        fills.extend([by] * n)
        return len(fills) - n

    SUBKEY_FILL = {0: reserve(2 * HEADS // 4, "act")}
    VECTOR_FILL = reserve(1, "act")
    NORM_FILL, SCORE_FILL = {}, {}
    NORM_FILL["mix0"] = reserve(2 * CH, "dve")
    NORM_FILL["ffn0"] = reserve(2 * CH, "act")
    SCORE_FILL[0] = reserve(HEADS, "act")
    SUBKEY_FILL[1] = reserve(2 * HEADS // 4, "act")
    NORM_FILL["kv"] = reserve(2 * CH, "dve")
    HEAD_FILL = reserve(PAIRS, "act")
    NORM_FILL["ffn1"] = reserve(2 * CH, "act")
    SCORE_FILL[1] = reserve(HEADS, "act")
    NORMS = ["mix0", "ffn0", "kv", "ffn1", "final"]

    def nth(by_list, n):
        return by_list[:n + 1].count(by_list[n])

    with ExitStack() as ctx:
        def sb(name, shape, dt=F32):
            return ctx.enter_context(nc.sbuf_tensor(name, shape, dt))

        def sem(name):
            return ctx.enter_context(nc.semaphore(name))

        ident = sb("ident", [P, P])
        keep = sb("keep", [P, P])
        hide = sb("hide", [P, 3 * P])
        later = sb("later", [P, P])
        minus1 = sb("minus1", [P, P])
        iota = sb("iota", [P, TOPK], U32)
        vec_rows = sb("vec_rows", [48, P])
        vecs = sb("vecs", [P, 48])
        gains = sb("gains", [P, 3, D])
        h = sb("h", [P, CH, D])
        xn = sb("xn", [P, CH, D])
        xT = sb("xT", [P, KT, T])
        stat = sb("stat", [P, 6, CH])
        wring = sb("wring", [P, W_RING, KT, COLS])
        subT = sb("subT", [P, 2 * HEADS, KEYS])
        queryT = sb("queryT", [P, 2, 2, T])
        scores = sb("scores", [P, NH, 2 * KEYS])
        srch = sb("srch", [P, 2 * KEYS])
        srch2 = sb("srch2", [P, 2 * KEYS])
        side_v = sb("side_v", [P, 2, TOPK])
        side_i = sb("side_i", [P, 2, TOPK], U32)
        cand = sb("cand", [P, TOPK * TOPK])
        cand2 = sb("cand2", [P, TOPK * TOPK])
        cand_i = sb("cand_i", [P, TOPK], U32)
        digit = sb("digit", [P, 2, TOPK], U32)
        pick = sb("pick", [P, 2, TOPK, TOPK])
        picked = sb("picked", [P, 2, TOPK])
        expert_f = sb("expert_f", [P, TOPK])
        expert = [sb(f"expert{b}", [P, TOPK], U32) for b in range(2)]
        top = [sb(f"top{b}", [P, TOPK]) for b in range(2)]
        negmax = sb("negmax", [P, 2])
        gate = [sb(f"gate{b}", [P, TOPK]) for b in range(2)]
        gate_sum = sb("gate_sum", [P, 2])
        gate_inv = sb("gate_inv", [P, 2])
        dots = [sb(f"dots{b}", [P, TOPK]) for b in range(2)]
        gelu = [sb(f"gelu{b}", [P, TOPK]) for b in range(2)]
        coef = [sb(f"coef{b}", [P, TOPK]) for b in range(2)]
        diag = sb("diag", [P, GROUP, P])
        rows = sb("rows", [P, U_SLOTS + V_SLOTS, D])
        u_row = [rows[:, j, :] for j in range(U_SLOTS)]
        v_row = [rows[:, U_SLOTS + j, :] for j in range(V_SLOTS)]
        flat = rows[:, :, :].rearrange("p s d -> p (s d)")
        place = [0]

        def carve(*dims):
            n = 1
            for d in dims:
                n *= d
            a = flat[:, place[0]:place[0] + n]
            place[0] += n
            names = "abcd"[:len(dims)]
            return a.rearrange(f"p ({' '.join(names)}) -> p {' '.join(names)}", **dict(zip(names, dims)))

        sub_rows = [carve(2 * HEADS, KD)]
        conv_h = carve(2, 2, T)
        conv_u = carve(2, 2, T + TAPS - 1)
        conv_y = carve(2, 2, T)
        gatedT = carve(KT, T)
        place[0] = 0
        kvT = carve(KT, T)
        mixT = carve(KT, T)
        keyT = carve(KT, T)
        qryT = carve(KT, T)
        value = carve(CH, D)
        headT = carve(KT, T)
        soft = carve(2, 2, 3 * P)
        notlog = carve(2, 2, 3 * P)
        sub_rows.append(carve(2 * HEADS, KD))
        assert place[0] <= (U_SLOTS + V_SLOTS) * D

        sums = ctx.enter_context(nc.psum_tensor("sums", [P, 4, 512], F32))
        block_ps = ctx.enter_context(nc.psum_tensor("block_ps", [P, 2, 512], F32))
        side = ctx.enter_context(nc.psum_tensor("side", [P, 2, 512], F32))

        x_loaded, vec_loaded, sub_loaded, gain_loaded = map(sem, ("x_loaded", "vec_loaded", "sub_loaded", "gain_loaded"))
        consts = sem("consts")
        w_landed = [sem(f"w_landed{j}") for j in range(W_RING)]
        u_landed = [sem(f"u_landed{j}") for j in range(U_SLOTS)]
        v_landed = [sem(f"v_landed{j}") for j in range(V_SLOTS)]
        block_done = sem("block_done")
        block_read = {"act": sem("block_read_by_act"), "dve": sem("block_read_by_dve")}
        side_done = sem("side_done")
        side_read = {"act": sem("side_read_by_act"), "dve": sem("side_read_by_dve")}
        dve_step = sem("dve_step")
        act_step = sem("act_step")
        squares = sem("squares")
        means = sem("means")
        estimates = sem("estimates")
        normed = sem("normed")
        expert_ready = sem("expert_ready")
        top_ready = sem("top_ready")
        gate_done = sem("gate_done")
        slot_clear = sem("slot_clear")
        search_clear = sem("search_clear")
        dot_done = sem("dot_done")
        gelu_done = sem("gelu_done")
        coef_ready = sem("coef_ready")
        diag_ready = sem("diag_ready")
        v_used = sem("v_used")
        head_added = sem("head_added")
        z_ready = sem("z_ready")
        log_done = sem("log_done")
        soft_ready = sem("soft_ready")
        expo_ready = sem("expo_ready")
        expo_read = sem("expo_read")
        weight_ready = sem("weight_ready")
        stored = sem("stored")

        block = ctx.enter_context(nc.Block())

        def wait_block_read(eng, m):
            eng.wait_ge(block_read[readers[m]], nth(readers, m))

        def wait_side_read(eng, n):
            eng.wait_ge(side_read[fills[n]], nth(fills, n))

        def input_of(norm):
            if norm == "mix0":
                return x_loaded, 16
            if norm in ("ffn0", "ffn1"):
                m = (W_OUT if norm == "ffn0" else W_O) + D // COLS - 1
                return block_read["dve"], nth(readers, m)
            return head_added, NH * (1 if norm == "kv" else 2)

        @block.sync
        def _(sp):
            for m, (w, col, _) in enumerate(blocks):
                if m >= W_RING:
                    sp.wait_ge(block_done, m - W_RING + 1)
                sp.dma_start(wring[:, m % W_RING],
                             w.rearrange("(k p) n -> p k n", p=P)[:, :, col:col + COLS]).then_inc(w_landed[m % W_RING], 16)
            for c in range(CH):
                sp.wait_ge(normed, CH * (len(NORMS) - 1) + c + 1)
                sp.dma_start(out[0, c * P:(c + 1) * P, :], xn[:, c, :]).then_inc(stored, 16)
            sp.wait_ge(stored, 16 * CH)

        @block.gpsimd
        def _(pool):
            nc.gpsimd.memset(ident[:], 0.0).then_inc(consts, 1)
            nc.gpsimd.memset(keep[:], 1.0).then_inc(consts, 1)
            nc.gpsimd.memset(hide[:], 0.0).then_inc(consts, 1)
            nc.gpsimd.memset(later[:], -1.0).then_inc(consts, 1)
            nc.gpsimd.memset(minus1[:], -1.0).then_inc(consts, 1)
            nc.gpsimd.iota(iota[:], pattern=[[1, TOPK]], base=0, channel_multiplier=0).then_inc(consts, 1)
            pool.wait_ge(consts, 6)
            nc.gpsimd.affine_select(out=ident[:], in_=ident[:], compare_op=ALU.not_equal, fill=1.0, base=0,
                                    pattern=[[-1, P]], channel_multiplier=1).then_inc(consts, 1)
            nc.gpsimd.affine_select(out=keep[:], in_=keep[:], compare_op=ALU.is_gt, fill=0.0, base=0,
                                    pattern=[[1, P]], channel_multiplier=-1).then_inc(consts, 1)
            for b in (0, 2):
                at = hide[:, b * P:(b + 1) * P]
                nc.gpsimd.affine_select(out=at, in_=at, compare_op=ALU.is_gt, fill=MASKED, base=0,
                                        pattern=[[1, P]], channel_multiplier=-1).then_inc(consts, 1)
            nc.gpsimd.affine_select(out=later[:], in_=later[:], compare_op=ALU.is_ge, fill=0.0, base=0,
                                    pattern=[[-1, P]], channel_multiplier=1).then_inc(consts, 1)

            u_table = peer_u.rearrange("l e d -> (l e) d")
            v_table = peer_v.rearrange("l e d -> (l e) d")

            def gather_pair(layer, i):
                for b in range(2):
                    n = NH * layer + 2 * i + b
                    pool.wait_ge(expert_ready, n + 1)
                    pool.sem_inc(slot_clear, 1)
                    for g in range(GROUPS):
                        for j in range(GROUP):
                            if not (isinstance(n, int) and n == 0 and g == 0):
                                pool.wait_ge(dot_done, GROUP * (GROUPS * n + g - 1) + j + 1)
                                pool.sem_inc(slot_clear, 1)
                            k = g * GROUP + j
                            pool.indirect_dma_start(
                                u_row[j], None, u_table,
                                bass.IndirectOffsetOnAxis(ap=expert[b][:, k:k + 1], axis=0)).then_inc(u_landed[j], 16)
                        for j in range(GROUP):
                            k = g * GROUP + j
                            if not (isinstance(n, int) and n == 0):
                                pool.wait_ge(v_used, TOPK * (n - 1) + k + 1)
                                pool.sem_inc(slot_clear, 1)
                            pool.indirect_dma_start(
                                v_row[k], None, v_table,
                                bass.IndirectOffsetOnAxis(ap=expert[b][:, k:k + 1], axis=0)).then_inc(v_landed[k], 16)

            for layer in range(LAYERS):
                gather_pair(layer, 0)
                with pool.Fori(1, NH // 2) as i:
                    gather_pair(layer, i)

        @block.tensor
        def _(pe):
            def take_side(n):
                if n >= 2:
                    wait_side_read(pe, n - 2)
                return side[:, n % 2, :]

            def take_block(m):
                pe.wait_ge(w_landed[m % W_RING], 16 * (m // W_RING + 1))
                if m >= 2:
                    wait_block_read(pe, m - 2)
                return wring[:, m % W_RING], block_ps[:, m % 2, :]

            def to_features(m, xt):
                w, bank = take_block(m)
                for s in range(2):
                    for k in range(KT):
                        last = nc.tensor.matmul(bank[:, s * T:(s + 1) * T], w[:, k, s * P:(s + 1) * P], xt[:, k, :],
                                                start=(k == 0), stop=(k == KT - 1))
                last.then_inc(block_done, 1)

            def to_tokens(m, xt):
                w, bank = take_block(m)
                for c in range(CH):
                    for k in range(KT):
                        last = nc.tensor.matmul(bank[:, c * COLS:(c + 1) * COLS], xt[:, k, c * P:(c + 1) * P], w[:, k, :],
                                                start=(k == 0), stop=(k == KT - 1))
                last.then_inc(block_done, 1)

            def transpose_norm(norm):
                for c in range(CH):
                    pe.wait_ge(normed, CH * NORMS.index(norm) + c + 1)
                    for half in range(2):
                        n = NORM_FILL[norm] + 2 * c + half
                        bank = take_side(n)
                        for q in range(4):
                            k = 4 * half + q
                            last = nc.tensor.transpose(bank[:, q * P:(q + 1) * P], xn[:, c, k * P:(k + 1) * P], ident[:])
                        last.then_inc(side_done, 1)

            def score_heads(layer, norm):
                wait_side_read(pe, NORM_FILL[norm] + 2 * CH - 1)

                def score(hd):
                    wait_block_read(pe, QUERY[layer] + hd)
                    bank = take_side(SCORE_FILL[layer] + hd)
                    for c in range(CH):
                        for p in range(2):
                            last = nc.tensor.matmul(bank[:, (2 * c + p) * P:(2 * c + p + 1) * P],
                                                    queryT[:, hd % 2, p, c * P:(c + 1) * P],
                                                    subT[:, 2 * hd + p, :], start=True, stop=True)
                    last.then_inc(side_done, 1)

                for hd in range(HEADS):
                    to_features(QUERY[layer] + hd, xT)
                    if hd >= 1:
                        score(hd - 1)
                score(HEADS - 1)

            def combine_pair(layer, i):
                for b in range(2):
                    n = NH * layer + 2 * i + b
                    if not (isinstance(n, int) and n < 2):
                        pe.wait_ge(head_added, n - 1)
                    for k in range(TOPK):
                        pe.wait_ge(diag_ready, TOPK * n + k + 1)
                        pe.wait_ge(v_landed[k], 16 * (n + 1))
                        for half in range(2):
                            last = nc.tensor.matmul(sums[:, 2 * b + half, :], diag[:, k % GROUP, :],
                                                    v_row[k][:, half * 512:(half + 1) * 512],
                                                    start=(k == 0), stop=(k == TOPK - 1))
                        last.then_inc(v_used, 1)

            def transpose_subkeys(layer):
                pe.wait_ge(sub_loaded, 16 * (layer + 1))
                for n in range(2 * HEADS // 4):
                    bank = take_side(SUBKEY_FILL[layer] + n)
                    for q in range(4):
                        last = nc.tensor.transpose(bank[:, q * P:(q + 1) * P], sub_rows[layer][:, 4 * n + q, :], ident[:])
                    last.then_inc(side_done, 1)

            pe.wait_ge(consts, 11)
            transpose_subkeys(0)
            pe.wait_ge(vec_loaded, 48)
            bank = take_side(VECTOR_FILL)
            nc.tensor.transpose(bank[:, 0:48], vec_rows[:, :], ident[0:48, 0:48]).then_inc(side_done, 1)

            transpose_norm("mix0")
            wait_side_read(pe, NORM_FILL["mix0"] + 2 * CH - 1)
            for m in range(CONV, W_OUT):
                to_features(m, xT)
            wait_block_read(pe, W_OUT - 1)
            for m in range(W_OUT, W_OUT + D // COLS):
                to_tokens(m, gatedT)
            transpose_norm("ffn0")
            score_heads(0, "ffn0")
            combine_pair(0, 0)
            with pe.Fori(1, NH // 2) as i:
                combine_pair(0, i)

            transpose_subkeys(1)
            transpose_norm("kv")
            wait_side_read(pe, NORM_FILL["kv"] + 2 * CH - 1)
            for m in range(W_K, W_V):
                to_features(m, kvT)
            for m in range(W_V, W_Q):
                to_tokens(m, kvT)
            for m in range(W_Q, W_O):
                to_features(m, mixT)
            wait_block_read(pe, W_O - 1)

            def logits(hp):
                if hp >= 2:
                    pe.wait_ge(expo_read, hp - 1)
                for e in range(2):
                    r = slice(e * DH, (e + 1) * DH)
                    bank = sums[:, 2 * (hp % 2) + e, :]
                    nc.tensor.matmul(bank[:, 0:T], keyT[r, hp, 0:P], qryT[r, hp, :], start=True, stop=True,
                                     skip_group_check=True)
                    last = nc.tensor.matmul(bank[:, T:T + P], keyT[r, hp, P:T], qryT[r, hp, P:T], start=False, stop=True,
                                            skip_group_check=True)
                last.then_inc(z_ready, 1)

            def exponents(hp):
                pe.wait_ge(soft_ready, hp + 1)
                for e in range(2):
                    bank, s = sums[:, 2 * (hp % 2) + e, :], notlog[:, hp % 2, e, :]
                    nc.tensor.matmul(bank[:, 0:T], later[:], s[:, 0:T], start=False, stop=True, skip_group_check=True)
                    nc.tensor.matmul(bank[:, P:T], minus1[:], s[:, T:T + P], start=False, stop=True, skip_group_check=True)
                    last = nc.tensor.matmul(bank[:, T:T + P], later[:], s[:, T:T + P], start=False, stop=True,
                                            skip_group_check=True)
                last.then_inc(expo_ready, 1)

            def heads_out(hp):
                pe.wait_ge(weight_ready, hp + 1)
                bank = take_side(HEAD_FILL + hp)
                for e in range(2):
                    o, w = bank[e * DH:(e + 1) * DH, :], soft[:, hp % 2, e, :]
                    v = value[:, :, (2 * hp + e) * DH:(2 * hp + e + 1) * DH]
                    nc.tensor.matmul(o[:, 0:T], v[:, 0, :], w[:, 0:T], start=True, stop=False, skip_group_check=True)
                    last = nc.tensor.matmul(o[:, P:T], v[:, 1, :], w[:, T:T + P], start=False, stop=True,
                                            skip_group_check=True)
                last.then_inc(side_done, 1)

            logits(0)
            logits(1)
            exponents(0)
            for hp in range(PAIRS):
                if hp + 2 < PAIRS:
                    logits(hp + 2)
                if hp + 1 < PAIRS:
                    exponents(hp + 1)
                heads_out(hp)
            wait_side_read(pe, HEAD_FILL + PAIRS - 1)
            for m in range(W_O, W_O + D // COLS):
                to_tokens(m, headT)
            transpose_norm("ffn1")
            score_heads(1, "ffn1")
            combine_pair(1, 0)
            with pe.Fori(1, NH // 2) as i:
                combine_pair(1, i)

        @block.scalar
        def _(act):
            act.dma_start(h[:, :, :], x[0].rearrange("(c p) d -> p c d", p=P)).then_inc(x_loaded, 16)

            def load_subkeys(layer):
                act.dma_start(sub_rows[layer], peer_subkeys[layer].rearrange("h s n d -> n (h s) d")).then_inc(sub_loaded, 16)

            load_subkeys(0)
            act.dma_start(vec_rows[0:2 * KT, :], norm_mix.rearrange("l (k p) -> (l k) p", p=P)).then_inc(vec_loaded, 16)
            act.dma_start(vec_rows[2 * KT:3 * KT, :], norm_kv.rearrange("(k p) -> k p", p=P)).then_inc(vec_loaded, 16)
            act.dma_start(vec_rows[3 * KT:6 * KT, :], conv_kernel[0].rearrange("t (k p) -> (t k) p", p=P)).then_inc(vec_loaded, 16)
            for n, g in enumerate((norm_ffn[0], norm_ffn[1], norm_final)):
                act.dma_start(gains[:, n, :], g.partition_broadcast(P)).then_inc(gain_loaded, 16)

            steps = [0]

            def own(ins):
                ins.then_inc(act_step, 1)
                steps[0] += 1
                act.wait_ge(act_step, steps[0])

            def read_side(n, dst, src=None):
                act.wait_ge(side_done, n + 1)
                nc.scalar.activation(dst, side[:, n % 2, :] if src is None else src, ACT.Copy).then_inc(side_read["act"], 1)

            def read_block(m, dst, src, scale=1.0):
                act.wait_ge(block_done, m + 1)
                nc.scalar.activation(dst, src, ACT.Copy, scale=scale).then_inc(block_read["act"], 1)

            def norm_sums(norm):
                s = NORMS.index(norm)
                act.wait_ge(*input_of(norm))
                for c in range(CH):
                    nc.scalar.activation(xn[:, c, :], h[:, c, :], ACT.Square, accum_out=stat[:, 0, c:c + 1]).then_inc(squares, 1)
                act.wait_ge(means, s + 1)
                own(nc.scalar.activation(stat[:, 2, :], stat[:, 1, :], ACT.Ln))
                nc.scalar.activation(stat[:, 3, :], stat[:, 2, :], ACT.Exp, scale=-0.5).then_inc(estimates, 1)

            def turned_subkeys(layer):
                for j in range(2 * HEADS // 4):
                    n = SUBKEY_FILL[layer] + j
                    read_side(n, subT[:, 4 * j:4 * j + 4, :], side[:, n % 2, :].rearrange("p (k t) -> p k t", t=P))

            def turned_norm(norm):
                for c in range(CH):
                    for half in range(2):
                        n = NORM_FILL[norm] + 2 * c + half
                        read_side(n, xT[:, 4 * half:4 * half + 4, c * P:(c + 1) * P],
                                  side[:, n % 2, :].rearrange("p (k t) -> p k t", t=P))

            def score_heads(layer):
                def score(hd):
                    n = SCORE_FILL[layer] + hd
                    read_side(n, scores[:, hd:hd + HEADS + 1:HEADS, :], side[:, n % 2, :].rearrange("p (c k) -> p c k", c=CH))

                for hd in range(HEADS):
                    m = QUERY[layer] + hd
                    if hd >= 2:
                        act.wait_ge(side_done, SCORE_FILL[layer] + hd - 1)
                    read_block(m, queryT[:, hd % 2], block_ps[:, m % 2, :].rearrange("p (s t) -> p s t", s=2))
                    if hd >= 1:
                        score(hd - 1)
                score(HEADS - 1)

            def gates(n, b):
                act.wait_ge(top_ready, n + 1)
                nc.scalar.activation(gate[b][:], top[b][:], ACT.Exp, bias=negmax[:, b:b + 1],
                                     accum_out=gate_sum[:, b:b + 1]).then_inc(gate_done, 1)

            def weigh_pair(layer, i, last=False):
                for b in range(2):
                    n = NH * layer + 2 * i + b
                    for g in range(GROUPS):
                        ks = slice(g * GROUP, (g + 1) * GROUP)
                        act.wait_ge(dot_done, TOPK * n + GROUP * (g + 1))
                        nc.scalar.activation(gelu[b][:, ks], dots[b][:, ks], ACT.Gelu).then_inc(gelu_done, 1)
                        act.wait_ge(coef_ready, GROUPS * n + g + 1)
                        for j in range(GROUP):
                            k = g * GROUP + j
                            if not (isinstance(n, int) and n == 0 and g == 0):
                                act.wait_ge(v_used, TOPK * n + k - GROUP + 1)
                            nc.scalar.activation(diag[:, j, :], ident[:], ACT.Copy, scale=coef[b][:, k:k + 1]).then_inc(diag_ready, 1)
                        if g == 0 and not (last and b == 1):
                            gates(n + 1, 1 - b)

            def weigh(layer):
                gates(NH * layer, 0)
                weigh_pair(layer, 0)
                with act.Fori(1, NH // 2 - 1) as i:
                    weigh_pair(layer, i)
                weigh_pair(layer, NH // 2 - 1, last=True)

            act.wait_ge(consts, 11)
            norm_sums("mix0")
            turned_subkeys(0)
            read_side(VECTOR_FILL, vecs[:, :], side[:, VECTOR_FILL % 2, 0:48])
            for j in range(D // COLS):
                m = CONV + 3 * j
                if j >= 2:
                    wait_block_read(act, CONV + 3 * (j - 2) + 1)
                read_block(m, conv_h[:, j % 2], block_ps[:, m % 2, :].rearrange("p (s t) -> p s t", s=2))
            norm_sums("ffn0")
            turned_norm("ffn0")
            score_heads(0)
            weigh(0)

            act.wait_ge(*input_of("kv"))
            load_subkeys(1)
            norm_sums("kv")
            turned_subkeys(1)
            for j in range(D // COLS):
                m = W_K + j
                read_block(m, keyT[:, 2 * j:2 * j + 2, :], block_ps[:, m % 2, :].rearrange("p (s t) -> p s t", s=2))
            for j in range(D // COLS):
                m = W_V + j
                read_block(m, value[:, :, j * COLS:(j + 1) * COLS], block_ps[:, m % 2, :].rearrange("p (c n) -> p c n", c=CH))
            for j in range(D // COLS):
                m = W_Q + j
                read_block(m, qryT[:, 2 * j:2 * j + 2, :], block_ps[:, m % 2, :].rearrange("p (s t) -> p s t", s=2),
                           scale=float(DH) ** -0.5)

            def logs(hp):
                act.wait_ge(z_ready, hp + 1)
                if hp >= 2:
                    act.wait_ge(side_done, HEAD_FILL + hp - 1)
                s = soft[:, hp % 2]
                own(nc.scalar.activation(s, sums[:, 2 * (hp % 2):2 * (hp % 2) + 2, 0:3 * P], ACT.Abs))
                own(nc.scalar.activation(s, s, ACT.Exp, scale=-1.0))
                nc.scalar.activation(s, s, ACT.Ln, bias=1.0).then_inc(log_done, 1)

            logs(0)
            logs(1)
            for hp in range(PAIRS):
                act.wait_ge(expo_read, hp + 1)
                nc.scalar.activation(soft[:, hp % 2], soft[:, hp % 2], ACT.Exp).then_inc(weight_ready, 1)
                if hp + 2 < PAIRS:
                    logs(hp + 2)
                n = HEAD_FILL + hp
                read_side(n, headT[:, hp, :], side[:, n % 2, 0:T])
            norm_sums("ffn1")
            turned_norm("ffn1")
            score_heads(1)
            weigh(1)
            norm_sums("final")

        @block.vector
        def _(dve):
            done = [0]

            def mark(ins):
                ins.then_inc(dve_step, 1)
                done[0] = done[0] + 1
                return done[0]

            def need(value):
                dve.wait_ge(dve_step, value)

            def need_apart(value):
                need(value)
                if not isinstance(value, int):
                    dve.sem_inc(search_clear, 1)

            def norm_stream(norm):
                s = NORMS.index(norm)
                mean, y, r, t = stat[:, 1, :], stat[:, 3, :], stat[:, 4, :], stat[:, 5, :]
                dve.wait_ge(squares, CH * (s + 1))
                nc.vector.tensor_scalar(mean, stat[:, 0, :], 1.0 / D, EPS, ALU.mult, ALU.add).then_inc(means, 1)
                dve.wait_ge(estimates, s + 1)
                need(mark(nc.vector.tensor_tensor(t, y, y, ALU.mult)))
                need(mark(nc.vector.tensor_tensor(t, t, mean, ALU.mult)))
                need(mark(nc.vector.tensor_scalar(t, t, -0.5, 1.5, ALU.mult, ALU.add)))
                need(mark(nc.vector.tensor_tensor(r, y, t, ALU.mult)))
                row = {"ffn0": 0, "ffn1": 1, "final": 2}.get(norm)
                if norm == "ffn0":
                    dve.wait_ge(gain_loaded, 48)
                for c in range(CH):
                    if row is None:
                        nc.vector.tensor_scalar(xn[:, c, :], h[:, c, :], r[:, c:c + 1], None, ALU.mult).then_inc(normed, 1)
                    else:
                        nc.vector.scalar_tensor_tensor(out=xn[:, c, :], in0=h[:, c, :], scalar=r[:, c:c + 1],
                                                       in1=gains[:, row, :], op0=ALU.mult, op1=ALU.mult).then_inc(normed, 1)

            def turned_norm(norm, outs):
                for c in range(CH):
                    for half in range(2):
                        n = NORM_FILL[norm] + 2 * c + half
                        dve.wait_ge(side_done, n + 1)
                        for t, (dst, col) in enumerate(outs):
                            g = vecs[:, col + 4 * half:col + 4 * half + 4].unsqueeze(2).to_broadcast([P, 4, P])
                            ins = nc.vector.tensor_tensor(dst[:, 4 * half:4 * half + 4, c * P:(c + 1) * P],
                                                          side[:, n % 2, :].rearrange("p (k t) -> p k t", t=P), g, ALU.mult)
                            if t == len(outs) - 1:
                                ins.then_inc(side_read["dve"], 1)

            def add_blocks(m0):
                for j in range(D // COLS):
                    m = m0 + j
                    dve.wait_ge(block_done, m + 1)
                    at = h[:, :, j * COLS:(j + 1) * COLS]
                    nc.vector.tensor_tensor(at, block_ps[:, m % 2, :].rearrange("p (c n) -> p c n", c=CH), at,
                                            ALU.add).then_inc(block_read["dve"], 1)

            def top16(values, indices, src, scratch, start):
                need_apart(start)
                a = mark(nc.vector.max(values[:, 0:8], src))
                need_apart(a)
                r = mark(nc.vector.match_replace(scratch, values[:, 0:8], src, FOUND))
                mark(nc.vector.max_index(indices[:, 0:8], values[:, 0:8], src))
                need_apart(r)
                b = mark(nc.vector.max(values[:, 8:16], scratch))
                need_apart(b)
                return mark(nc.vector.max_index(indices[:, 8:16], values[:, 8:16], scratch))

            def find_experts(n, at, b, layer):
                s = mark(nc.vector.tensor_copy(srch[:], scores[:, bass.ds(at, 1), :].rearrange("p a k -> p (a k)")))
                for p in range(2):
                    e = top16(side_v[:, p, :], side_i[:, p, :], srch[:, p * KEYS:(p + 1) * KEYS],
                              srch2[:, p * KEYS:(p + 1) * KEYS], s)
                need(e)
                c = mark(nc.vector.tensor_tensor(cand[:].rearrange("p (a b) -> p a b", b=TOPK),
                                                 side_v[:, 0, :].unsqueeze(2).to_broadcast([P, TOPK, TOPK]),
                                                 side_v[:, 1, :].unsqueeze(1).to_broadcast([P, TOPK, TOPK]), ALU.add))
                e = top16(top[b][:], cand_i[:], cand[:], cand2[:], c)
                need(e)
                nc.vector.tensor_scalar(negmax[:, b:b + 1], top[b][:, 0:1], -1.0, None, ALU.mult).then_inc(top_ready, 1)
                mark(nc.vector.tensor_scalar(digit[:, 0, :], cand_i[:], 4, None, ALU.logical_shift_right))
                d = mark(nc.vector.tensor_scalar(digit[:, 1, :], cand_i[:], TOPK - 1, None, ALU.bitwise_and))
                need(d)
                d = mark(nc.vector.tensor_tensor(pick[:].rearrange("p a k j -> p (a k) j"),
                                                 digit[:].rearrange("p a k -> p (a k)").unsqueeze(2).to_broadcast([P, 2 * TOPK, TOPK]),
                                                 iota[:].unsqueeze(1).to_broadcast([P, 2 * TOPK, TOPK]), ALU.is_equal))
                need(d)
                d = mark(nc.vector.tensor_tensor(pick[:], pick[:],
                                                 side_i[:].unsqueeze(2).to_broadcast([P, 2, TOPK, TOPK]), ALU.mult))
                need(d)
                d = mark(nc.vector.tensor_reduce(picked[:].rearrange("p a k -> p (a k)"),
                                                 pick[:].rearrange("p a k j -> p (a k) j"), AX_X, ALU.add))
                need(d)
                d = mark(nc.vector.scalar_tensor_tensor(out=expert_f[:], in0=picked[:, 0, :], scalar=float(KEYS),
                                                        in1=picked[:, 1, :], op0=ALU.mult, op1=ALU.add))
                need(d)
                nc.vector.tensor_scalar(expert[b][:], expert_f[:], float(layer * EXPERTS), None, ALU.add).then_inc(expert_ready, 1)

            def dot_group(n, chunk, b, g):
                for j in range(GROUP):
                    k = g * GROUP + j
                    dve.wait_ge(u_landed[j], 16 * (GROUPS * n + g + 1))
                    nc.vector.scalar_tensor_tensor(out=u_row[j], in0=u_row[j], scalar=1.0,
                                                   in1=xn[:, bass.ds(chunk, 1), :].rearrange("p c d -> p (c d)"),
                                                   op0=ALU.mult, op1=ALU.mult,
                                                   accum_out=dots[b][:, k:k + 1]).then_inc(dot_done, 1)

            def add_head(n, chunk, b):
                dve.wait_ge(v_used, TOPK * (n + 1))
                at = h[:, bass.ds(chunk, 1), :].rearrange("p c d -> p (c d)")
                nc.vector.tensor_tensor(at, sums[:, 2 * b:2 * b + 2, :].rearrange("p a d -> p (a d)"), at,
                                        ALU.add).then_inc(head_added, 1)

            def coefficients(n, b, g):
                dve.wait_ge(gelu_done, GROUPS * n + g + 1)
                if g == 0:
                    dve.wait_ge(gate_done, n + 1)
                    need(mark(nc.vector.reciprocal(gate_inv[:, b:b + 1], gate_sum[:, b:b + 1])))
                ks = slice(g * GROUP, (g + 1) * GROUP)
                nc.vector.scalar_tensor_tensor(out=coef[b][:, ks], in0=gelu[b][:, ks], scalar=gate_inv[:, b:b + 1],
                                               in1=gate[b][:, ks], op0=ALU.mult, op1=ALU.mult).then_inc(coef_ready, 1)

            def expert_pair(layer, i, last=False):
                for b in range(2):
                    at = 2 * i + b
                    n = NH * layer + at
                    chunk = i // (HEADS // 2)
                    first = isinstance(i, int) and i == 0
                    dot_group(n, chunk, b, 0)
                    if not (first and b == 0):
                        add_head(n - 1, (2 * i - 1) // HEADS if b == 0 else chunk, 1 - b)
                    if not (last and b == 1):
                        if first:
                            wait_side_read(dve, SCORE_FILL[layer] + at + 1)
                        find_experts(n + 1, at + 1, 1 - b, layer)
                    coefficients(n, b, 0)
                    dot_group(n, chunk, b, 1)
                    coefficients(n, b, 1)

            def experts(layer):
                wait_side_read(dve, SCORE_FILL[layer])
                find_experts(NH * layer, 0, 0, layer)
                before = done[0]
                expert_pair(layer, 0)
                per = done[0] - before
                wait_side_read(dve, SCORE_FILL[layer] + HEADS - 1)
                start, rounds = done[0], NH // 2 - 2
                with dve.Fori(1, 1 + rounds) as i:
                    done[0] = start - per + per * i
                    expert_pair(layer, i)
                done[0] = start + per * rounds
                expert_pair(layer, NH // 2 - 1, last=True)
                add_head(NH * layer + NH - 1, CH - 1, 1)

            for b in range(2):
                mark(nc.vector.memset(conv_u[:, b, :, 0:TAPS - 1], 0.0))
            norm_stream("mix0")
            wait_side_read(dve, VECTOR_FILL)
            turned_norm("mix0", [(xT, 0)])
            for j in range(D // COLS):
                m_h, m_c, m_b = (CONV + 3 * j + t for t in range(3))
                u, y = conv_u[:, j % 2], conv_y[:, j % 2]
                banks = {m: block_ps[:, m % 2, :].rearrange("p (s t) -> p s t", s=2) for m in (m_c, m_b)}
                wait_block_read(dve, m_h)
                dve.wait_ge(block_done, m_c + 1)
                nc.vector.tensor_tensor(u[:, :, TAPS - 1:], banks[m_c], conv_h[:, j % 2], ALU.mult).then_inc(block_read["dve"], 1)
                wait_block_read(dve, m_c)
                tap = lambda i, s: vecs[:, (3 + i) * KT + 2 * j + s:(3 + i) * KT + 2 * j + s + 1]
                for i in range(TAPS):
                    for s in range(2):
                        src = u[:, s, i:i + T]
                        if i == 0:
                            e = mark(nc.vector.tensor_scalar(y[:, s, :], src, tap(i, s), None, ALU.mult))
                        else:
                            need(e_of[s])
                            e = mark(nc.vector.scalar_tensor_tensor(out=y[:, s, :], in0=src, scalar=tap(i, s), in1=y[:, s, :],
                                                                    op0=ALU.mult, op1=ALU.add))
                        if i == 0 and s == 0:
                            e_of = [0, 0]
                        e_of[s] = e
                need(e)
                dve.wait_ge(block_done, m_b + 1)
                nc.vector.tensor_tensor(gatedT[:, 2 * j:2 * j + 2, :], banks[m_b], y, ALU.mult).then_inc(block_read["dve"], 1)
            add_blocks(W_OUT)
            norm_stream("ffn0")
            experts(0)

            norm_stream("kv")
            turned_norm("kv", [(kvT, 2 * KT), (mixT, KT)])

            def banks_of(hp):
                return sums[:, 2 * (hp % 2):2 * (hp % 2) + 2, 0:3 * P]

            def softplus(hp):
                dve.wait_ge(log_done, hp + 1)
                s = notlog[:, hp % 2]
                need(mark(nc.vector.scalar_tensor_tensor(out=s, in0=banks_of(hp), scalar=0.0, in1=soft[:, hp % 2],
                                                         op0=ALU.max, op1=ALU.add)))
                for e in range(2):
                    d = s[:, e, :].rearrange("p (b t) -> p b t", t=P)[:, 0:3:2, :]
                    ins = nc.vector.tensor_tensor(d, d, keep[:].unsqueeze(1).to_broadcast([P, 2, P]), ALU.mult)
                ins.then_inc(soft_ready, 1)

            def exponent(hp):
                dve.wait_ge(expo_ready, hp + 1)
                nc.vector.scalar_tensor_tensor(out=soft[:, hp % 2], in0=banks_of(hp), scalar=0.0,
                                               in1=hide[:].unsqueeze(1).to_broadcast([P, 2, 3 * P]),
                                               op0=ALU.min, op1=ALU.add).then_inc(expo_read, 1)

            softplus(0)
            for hp in range(PAIRS):
                if hp + 1 < PAIRS:
                    softplus(hp + 1)
                exponent(hp)
            add_blocks(W_O)
            norm_stream("ffn1")
            experts(1)
            norm_stream("final")


_INS = ["x", "norm_mix", "norm_ffn", "conv_w_in", "conv_kernel", "conv_w_out", "norm_kv", "w_kv", "attn_w_q",
        "attn_w_o", "peer_w_query", "peer_subkeys", "peer_u", "peer_v", "norm_final"]


def kernel(**inputs):
    import numpy as _np
    import concourse.bacc as _bacc
    from concourse import mybir as _mybir
    from concourse.bass_utils import run_bass_kernel_spmd as _run

    nc = _bacc.Bacc("TRN2", target_bir_lowering=False, num_devices=1)
    arrays, args = {}, []
    for name in _INS:
        a = _np.ascontiguousarray(inputs[name])
        arrays[f"in_{name}"] = a
        args.append(nc.dram_tensor(f"in_{name}", a.shape, _mybir.dt.from_np(a.dtype), kind="ExternalInput").ap())
    shape = inputs["x"].shape
    args.append(nc.dram_tensor("out_stream", shape, _mybir.dt.float32, kind="ExternalOutput").ap())
    trunk(nc, *args)
    r = _run(nc, [arrays], core_ids=[0])
    return r.results[0]["out_stream"]
```

```python
from contextlib import ExitStack

import concourse.bass as bass
from concourse import mybir

F32 = mybir.dt.float32
U32 = mybir.dt.uint32
ALU = mybir.AluOpType
ACT = mybir.ActivationFunctionType
AX_X = mybir.AxisListType.X

P = 128
EPS = 1e-6
FOUND = -3.0e38
MASKED = -1.0e4
COLS = 256
W_RING = 3
W_EARLY = 3
U_SLOTS = 8
V_SLOTS = 16
GROUP = 8


def trunk(nc, x, norm_mix, norm_ffn, conv_w_in, conv_kernel, conv_w_out, norm_kv, w_kv,
          attn_w_q, attn_w_o, peer_w_query, peer_subkeys, peer_u, peer_v, norm_final, out):
    _, T, D = x.shape
    LAYERS, HEADS, _, KEYS, KD = peer_subkeys.shape
    EXPERTS = peer_u.shape[1]
    TAPS = conv_kernel.shape[1]
    CH = T // P
    KT = D // P
    TOPK = 16
    DH = 64
    PAIRS = D // (2 * DH)
    NH = CH * HEADS
    STEPS = LAYERS * NH
    GROUPS = TOPK // GROUP
    assert (CH, KEYS, KD, COLS) == (2, P, P, 2 * P) and GROUPS == 2 and D == PAIRS * P and KT == PAIRS
    assert U_SLOTS == GROUP and V_SLOTS == TOPK and TAPS == 3 and LAYERS == 2

    NB = D // COLS
    SLOTS = HEADS * GROUPS
    fills, FILL = [], {}
    turn = {"block": [0, 1], "side": [2, 3]}

    def fill(by, bank, *name):
        if bank in turn:
            turn[bank].reverse()
            bank = turn[bank][1]
        FILL[name] = len(fills)
        fills.append((by, bank))

    for q in range(2 * HEADS // 4):
        fill("act", "side", "subkeys", 0, q)
    fill("act", "side", "vectors")
    for c in range(CH):
        for half in range(2):
            fill("dve", "side", "turn", "mix0", c, half)
    for j in range(NB):
        for part, by in ((2, "act"), (1, "dve"), (0, "dve")):
            fill(by, "block", "conv", j, part)
    for c in range(CH):
        for half in range(2):
            fill("act", "side", "turn", "ffn0", c, half)
        fill("act", "block", "query", 0, c, 0)
        fill("act", "side", "score", 0, c, 0)
    fill("act", "block", "query", 0, "both", 1)
    for hd in range(2, HEADS + 1):
        if hd < HEADS:
            fill("act", "block", "query", 0, "both", hd)
        fill("act", "side", "score", 0, "both", hd - 1)

    def fills_of_heads(c, hd):
        if hd < HEADS:
            fill("act", "block", "query", 1, c, hd)
        fill("act", "side", "score", 1, c, hd - 1)

    def fills_of_slot(c, t):
        for name, j in PROJECTED.get(t, []):
            if name in ("z", "heads"):
                if name == "z":
                    for e in range(2):
                        fill("dve", 2 + e, "z", c, j, e)
                else:
                    fill("act", "block", "heads", c, j)
            else:
                fill("act", "block", name, c, j)

    PROJECTED = {1: [("key", 0), ("qry", 0), ("val", 0)], 2: [("z", 0), ("key", 1), ("qry", 1)],
                 3: [("val", 1), ("key", 2)], 4: [("heads", 0), ("z", 1), ("qry", 2), ("val", 2)],
                 5: [("key", 3), ("qry", 3)], 6: [("heads", 1), ("z", 2), ("val", 3)],
                 8: [("heads", 2), ("z", 3)], 10: [("heads", 3)]}
    assert NB == 4 and SLOTS == 16 and HEADS == 8
    for c in range(CH):
        for t in range(SLOTS + 1):
            if t == SLOTS and c == 0:
                continue
            if t in (0, SLOTS) and (c == 1):
                for hd in (6, 7, 8):
                    fills_of_heads(0 if t == 0 else 1, hd)
            if t == 0:
                for half in range(2):
                    fill("dve", "side", "turn", "kv", c, half)
            fills_of_slot(c, t)
            if t == 7 and c == 0:
                for q in range(2 * HEADS // 4):
                    fill("act", "block", "subkeys", 1, q)
            if t in (10, 11):
                for q in (0, 1):
                    fill("dve", 2 * (t - 10) + q, "out", c, 2 * (t - 10) + q)
            if t == 12:
                for half in range(2):
                    fill("act", "side", "turn", "ffn1", c, half)
                fill("act", "block", "query", 1, c, 0)
            if t in (13, 14, 15):
                for hd in {13: [1], 14: [2, 3], 15: [4, 5]}[t]:
                    fills_of_heads(c, hd)

    def nth(n):
        by = fills[n][0]
        return sum(f[0] == by for f in fills[:n + 1])

    blocks, BLOCK, freed_by = [], {}, []

    def stream(w, col, freed, *name):
        BLOCK[name] = len(blocks)
        blocks.append((w, col))
        freed_by.append(freed)

    stream(peer_subkeys[0], None, FILL["subkeys", 0, 3], "subkeys", 0)
    for j in range(NB):
        for part in (2, 1, 0):
            stream(conv_w_in[0], part * D + j * COLS, FILL["conv", j, part], "conv", j, part)
    for q in range(NB):
        stream(conv_w_out[0], q * COLS, ("half", q // 2), "out0", q)
    for hd in range(HEADS):
        stream(peer_w_query[0], hd * COLS, FILL["query", 0, "both" if hd else 1, hd], "query", 0, "both", hd)
    for c in range(CH):
        for t in sorted(PROJECTED):
            for name, j in PROJECTED[t]:
                if name in ("key", "qry", "val"):
                    w, first = {"key": (w_kv, 0), "qry": (attn_w_q[0], 0), "val": (w_kv, D)}[name]
                    stream(w, first + j * COLS, FILL[name, c, j], name, c, j)
            if t == 6 and c == 0:
                stream(peer_subkeys[1], None, FILL["subkeys", 1, 3], "subkeys", 1)
        for q in range(NB):
            stream(attn_w_o[0], q * COLS, FILL["out", c, q], "out", c, q)
        for hd in range(HEADS):
            stream(peer_w_query[1], hd * COLS, FILL["query", 1, c, hd], "query", 1, c, hd)
    early = BLOCK["out0", NB - 1] + 1
    w_slot = [m % (W_RING + W_EARLY) if m < early else (m - early) % W_RING for m in range(len(blocks))]

    def before_in_slot(m):
        earlier = [b for b in range(m) if w_slot[b] == w_slot[m]]
        return (earlier[-1] if earlier else None), len(earlier)

    NORM_ORDER = [("mix0", 0), ("mix0", 1), ("ffn0", 0), ("ffn0", 1), ("kv", 0), ("ffn1", 0), ("kv", 1), ("ffn1", 1),
                  ("final", 0), ("final", 1)]

    with ExitStack() as ctx:
        def sb(name, shape, dt=F32):
            return ctx.enter_context(nc.sbuf_tensor(name, shape, dt))

        def sem(name):
            return ctx.enter_context(nc.semaphore(name))

        ident = sb("ident", [P, P])
        keep = sb("keep", [P, P])
        hide = sb("hide", [P, P])
        later = sb("later", [P, P])
        minus1 = sb("minus1", [P, P])
        iota = sb("iota", [P, TOPK], U32)
        vec_rows = sb("vec_rows", [48, P])
        vecs = sb("vecs", [P, 48])
        gain = sb("gain", [P, D])
        h = sb("h", [P, CH, D])
        xn = sb("xn", [P, CH, D])
        xT = sb("xT", [P, KT, T])
        stat = sb("stat", [P, 6, CH])
        wring = sb("wring", [P, W_RING, KT, COLS])
        subT = sb("subT", [P, 2 * HEADS, KEYS])
        scores = sb("scores", [P, NH, 2 * KEYS])
        find = sb("find", [P, 4 * KEYS])
        srch = cand = find[:, 0:2 * KEYS]
        srch2 = cand2 = find[:, 2 * KEYS:4 * KEYS]
        pick = find[:, :].rearrange("p (a k j) -> p a k j", a=2, j=TOPK)
        side_v = sb("side_v", [P, 2, TOPK])
        side_i = sb("side_i", [P, 2, TOPK], U32)
        cand_i = sb("cand_i", [P, TOPK], U32)
        digit = sb("digit", [P, 2, TOPK], U32)
        picked = sb("picked", [P, 2, TOPK])
        expert_f = sb("expert_f", [P, TOPK])
        expert = [sb(f"expert{b}", [P, TOPK], U32) for b in range(2)]
        top = [sb(f"top{b}", [P, TOPK]) for b in range(2)]
        negmax = sb("negmax", [P, 2])
        gate = [sb(f"gate{b}", [P, TOPK]) for b in range(2)]
        gate_sum = sb("gate_sum", [P, 2])
        gate_inv = sb("gate_inv", [P, 2])
        dots = [sb(f"dots{b}", [P, TOPK]) for b in range(2)]
        gelu = [sb(f"gelu{b}", [P, TOPK]) for b in range(2)]
        coef = [sb(f"coef{b}", [P, TOPK]) for b in range(2)]
        diag = sb("diag", [P, GROUP, P])
        keyT = sb("keyT", [P, KT, T])
        value = sb("value", [P, CH, D])
        soft = sb("soft", [P, 2, 4 * P])
        notlog = sb("notlog", [P, 2, 4 * P])
        queryT = soft[:, :, :].rearrange("p b (s t) -> p b s t", t=T)
        kvT, mixT = xT[:, :, 0:P], xT[:, :, P:T]

        def work(c, part):
            a = scores[:, c * HEADS + part * HEADS // 2:c * HEADS + (part + 1) * HEADS // 2, :]
            return a.rearrange("p a k -> p (a k)").rearrange("p (k t) -> p k t", t=P)

        qryT = [work(c, 0) for c in range(CH)]
        headT = [work(c, 1) for c in range(CH)]
        rows = sb("rows", [P, U_SLOTS + V_SLOTS, D])
        u_row = [rows[:, j, :] for j in range(U_SLOTS)]
        v_row = [rows[:, U_SLOTS + j, :] for j in range(V_SLOTS)]
        flat = rows[:, :, :].rearrange("p s d -> p (s d)")
        place = [0]

        def carve(*dims):
            n = 1
            for d in dims:
                n *= d
            a = flat[:, place[0]:place[0] + n]
            place[0] += n
            names = "abcd"[:len(dims)]
            return a.rearrange(f"p ({' '.join(names)}) -> p {' '.join(names)}", **dict(zip(names, dims)))

        conv_h = carve(2, 2, T)
        conv_u = carve(2, 2, T + TAPS - 1)
        conv_y = carve(2, 2, T)
        place[0] = (U_SLOTS + GROUP) * D
        gatedT = carve(KT, T)
        wearly = [carve(KT, COLS) for _ in range(W_EARLY)]
        assert place[0] <= (U_SLOTS + V_SLOTS) * D
        w_place = [wring[:, j] for j in range(W_RING)] + wearly

        sums = ctx.enter_context(nc.psum_tensor("sums", [P, 4, 512], F32))
        banks = ctx.enter_context(nc.psum_tensor("banks", [P, 4, 512], F32))

        def bank_of(*name):
            return banks[:, fills[FILL[name]][1], :]

        x_loaded = [sem(f"x_loaded{c}") for c in range(CH)]
        vec_loaded, gain_loaded = map(sem, ("vec_loaded", "gain_loaded"))
        consts = sem("consts")
        w_landed = [sem(f"w_landed{j}") for j in range(W_RING + W_EARLY)]
        u_landed = [sem(f"u_landed{j}") for j in range(U_SLOTS)]
        v_landed = [sem(f"v_landed{j}") for j in range(V_SLOTS)]
        bank_done = sem("bank_done")
        bank_read = {"act": sem("bank_read_by_act"), "dve": sem("bank_read_by_dve")}
        dve_step = sem("dve_step")
        act_step = sem("act_step")
        squares = sem("squares")
        means = sem("means")
        estimates = sem("estimates")
        normed = sem("normed")
        expert_ready = sem("expert_ready")
        top_ready = sem("top_ready")
        gate_done = sem("gate_done")
        slot_clear = sem("slot_clear")
        search_clear = sem("search_clear")
        dot_done = sem("dot_done")
        gelu_done = sem("gelu_done")
        coef_ready = sem("coef_ready")
        diag_ready = sem("diag_ready")
        v_used = sem("v_used")
        head_added = sem("head_added")
        out_done = sem("out_done")
        out_added = sem("out_added")
        log_done = sem("log_done")
        soft_ready = sem("soft_ready")
        expo_ready = sem("expo_ready")
        weight_ready = sem("weight_ready")
        stored = sem("stored")

        block = ctx.enter_context(nc.Block())

        def wait_filled(eng, *name):
            eng.wait_ge(bank_done, FILL[name] + 1)

        def wait_read(eng, *name):
            n = FILL[name]
            eng.wait_ge(bank_read[fills[n][0]], nth(n))

        def wait_input(eng, norm, c):
            if norm == "mix0":
                eng.wait_ge(x_loaded[c], 16)
            elif norm == "ffn0":
                eng.wait_ge(out_added, 2 * (c + 1))
            elif norm == "ffn1":
                wait_read(eng, "out", c, NB - 1)
            else:
                eng.wait_ge(head_added, NH * (norm == "final") + HEADS * (c + 1))

        def normed_count(norm, c):
            return NORM_ORDER.index((norm, c)) + 1

        @block.sync
        def _(sp):
            for c in range(CH):
                sp.dma_start(h[:, c, :], x[0, c * P:(c + 1) * P, :]).then_inc(x_loaded[c], 16)
            sp.dma_start(vec_rows[0:2 * KT, :], norm_mix.rearrange("l (k p) -> (l k) p", p=P)).then_inc(vec_loaded, 16)
            sp.dma_start(vec_rows[2 * KT:3 * KT, :], norm_kv.rearrange("(k p) -> k p", p=P)).then_inc(vec_loaded, 16)
            sp.dma_start(vec_rows[3 * KT:6 * KT, :], conv_kernel[0].rearrange("t (k p) -> (t k) p", p=P)).then_inc(vec_loaded, 16)
            for m, (w, col) in enumerate(blocks):
                before, _ = before_in_slot(m)
                if before is not None:
                    if isinstance(freed_by[before], tuple):
                        sp.wait_ge(out_done, 2 * (CH - 1) + freed_by[before][1] + 1)
                    else:
                        sp.wait_ge(bank_done, freed_by[before] + 1)
                at = w_place[w_slot[m]]
                if col is None:
                    sp.dma_start(at.rearrange("p k n -> p (k n)").rearrange("p (k n) -> p k n", n=KD),
                                 w.rearrange("h s n d -> n (h s) d")).then_inc(w_landed[w_slot[m]], 16)
                else:
                    sp.dma_start(at, w.rearrange("(k p) n -> p k n", p=P)[:, :, col:col + COLS]).then_inc(w_landed[w_slot[m]], 16)
            for c in range(CH):
                sp.wait_ge(normed, normed_count("final", c))
                sp.dma_start(out[0, c * P:(c + 1) * P, :], xn[:, c, :]).then_inc(stored, 16)
            sp.wait_ge(stored, 16 * CH)

        @block.gpsimd
        def _(pool):
            nc.gpsimd.memset(ident[:], 0.0).then_inc(consts, 1)
            nc.gpsimd.memset(keep[:], 1.0).then_inc(consts, 1)
            nc.gpsimd.memset(hide[:], 0.0).then_inc(consts, 1)
            nc.gpsimd.memset(later[:], -1.0).then_inc(consts, 1)
            nc.gpsimd.memset(minus1[:], -1.0).then_inc(consts, 1)
            nc.gpsimd.iota(iota[:], pattern=[[1, TOPK]], base=0, channel_multiplier=0).then_inc(consts, 1)
            pool.wait_ge(consts, 6)
            nc.gpsimd.affine_select(out=ident[:], in_=ident[:], compare_op=ALU.not_equal, fill=1.0, base=0,
                                    pattern=[[-1, P]], channel_multiplier=1).then_inc(consts, 1)
            nc.gpsimd.affine_select(out=keep[:], in_=keep[:], compare_op=ALU.is_gt, fill=0.0, base=0,
                                    pattern=[[1, P]], channel_multiplier=-1).then_inc(consts, 1)
            nc.gpsimd.affine_select(out=hide[:], in_=hide[:], compare_op=ALU.is_gt, fill=MASKED, base=0,
                                    pattern=[[1, P]], channel_multiplier=-1).then_inc(consts, 1)
            nc.gpsimd.affine_select(out=later[:], in_=later[:], compare_op=ALU.is_ge, fill=0.0, base=0,
                                    pattern=[[-1, P]], channel_multiplier=1).then_inc(consts, 1)

            u_table = peer_u.rearrange("l e d -> (l e) d")
            v_table = peer_v.rearrange("l e d -> (l e) d")

            def gather_pair(i):
                for b in range(2):
                    n = 2 * i + b
                    pool.wait_ge(expert_ready, n + 1)
                    pool.sem_inc(slot_clear, 1)
                    for g in range(GROUPS):
                        for j in range(GROUP):
                            if not (isinstance(n, int) and n == 0 and g == 0):
                                pool.wait_ge(dot_done, GROUP * (GROUPS * n + g - 1) + j + 1)
                                pool.sem_inc(slot_clear, 1)
                            k = g * GROUP + j
                            pool.indirect_dma_start(
                                u_row[j], None, u_table,
                                bass.IndirectOffsetOnAxis(ap=expert[b][:, k:k + 1], axis=0)).then_inc(u_landed[j], 16)
                        for j in range(GROUP):
                            k = g * GROUP + j
                            if isinstance(n, int) and n == 0:
                                if k == GROUP:
                                    pool.wait_ge(out_done, 2 * CH)
                                    pool.sem_inc(slot_clear, 1)
                            else:
                                pool.wait_ge(v_used, TOPK * (n - 1) + k + 1)
                                pool.sem_inc(slot_clear, 1)
                            pool.indirect_dma_start(
                                v_row[k], None, v_table,
                                bass.IndirectOffsetOnAxis(ap=expert[b][:, k:k + 1], axis=0)).then_inc(v_landed[k], 16)

            gather_pair(0)
            with pool.Fori(1, STEPS // 2) as i:
                gather_pair(i)

        @block.tensor
        def _(pe):
            taken = [0]

            def take(*name):
                n = FILL[name]
                assert n == taken[0], name
                taken[0] += 1
                before = [f for f in range(n) if fills[f][1] == fills[n][1]]
                if before:
                    pe.wait_ge(bank_read[fills[before[-1]][0]], nth(before[-1]))
                return banks[:, fills[n][1], :]

            def weights_of(*name):
                m = BLOCK[name]
                pe.wait_ge(w_landed[w_slot[m]], 16 * (before_in_slot(m)[1] + 1))
                return w_place[w_slot[m]]

            def to_features(bank, w, xt, tokens):
                for s in range(2):
                    for k in range(KT):
                        last = nc.tensor.matmul(bank[:, s * tokens:(s + 1) * tokens], w[:, k, s * P:(s + 1) * P], xt[:, k, :],
                                                start=(k == 0), stop=(k == KT - 1))
                last.then_inc(bank_done, 1)

            def to_tokens(bank, w, xt):
                for k in range(KT):
                    last = nc.tensor.matmul(bank, xt[:, k, :], w[:, k, :], start=(k == 0), stop=(k == KT - 1))
                return last

            def out_half(c, half):
                for q in range(2):
                    last = to_tokens(sums[:, 2 * c + half, q * COLS:(q + 1) * COLS], weights_of("out0", 2 * half + q),
                                     gatedT[:, :, c * P:(c + 1) * P])
                last.then_inc(out_done, 1)

            def transpose_norm(norm, c):
                pe.wait_ge(normed, normed_count(norm, c))
                for half in range(2):
                    bank = take("turn", norm, c, half)
                    for q in range(4):
                        k = 4 * half + q
                        last = nc.tensor.transpose(bank[:, q * P:(q + 1) * P], xn[:, c, k * P:(k + 1) * P], ident[:])
                    last.then_inc(bank_done, 1)

            def query(layer, c, hd):
                xt, n = (xT[:, :, :], T) if c == "both" else (xT[:, :, c * P:(c + 1) * P] if layer == 0 else kvT, P)
                to_features(take("query", layer, c, hd),
                            weights_of("query", layer, "both" if layer == 0 else c, hd), xt, n)

            def score(layer, c, hd):
                wait_read(pe, "query", layer, c, hd)
                bank = take("score", layer, c, hd)
                for at in range(CH if c == "both" else 1):
                    for p in range(2):
                        last = nc.tensor.matmul(bank[:, (2 * at + p) * P:(2 * at + p + 1) * P],
                                                queryT[:, hd % 2, p, at * P:(at + 1) * P], subT[:, 2 * hd + p, :],
                                                start=True, stop=True)
                last.then_inc(bank_done, 1)

            def combine(n, b, g):
                if g == 0 and not (isinstance(n, int) and n < 2):
                    pe.wait_ge(head_added, n - 1)
                for k in range(g * GROUP, (g + 1) * GROUP):
                    pe.wait_ge(diag_ready, TOPK * n + k + 1)
                    pe.wait_ge(v_landed[k], 16 * (n + 1))
                    for half in range(2):
                        last = nc.tensor.matmul(sums[:, 2 * b + half, :], diag[:, k % GROUP, :],
                                                v_row[k][:, half * 512:(half + 1) * 512],
                                                start=(k == 0), stop=(k == TOPK - 1))
                    last.then_inc(v_used, 1)

            def combine_pair(i):
                for b in range(2):
                    for g in range(GROUPS):
                        combine(2 * i + b, b, g)

            def transpose_subkeys(layer):
                raw = weights_of("subkeys", layer).rearrange("p k n -> p (k n)")
                for n in range(2 * HEADS // 4):
                    bank = take("subkeys", layer, n)
                    for q in range(4):
                        r = 4 * n + q
                        last = nc.tensor.transpose(bank[:, q * P:(q + 1) * P], raw[:, r * KD:(r + 1) * KD], ident[:])
                    last.then_inc(bank_done, 1)

            def logits(c, j):
                for e in range(2):
                    bank, r = take("z", c, j, e), slice(e * DH, (e + 1) * DH)
                    for blk in range(1 - c, 2):
                        kc = c - 1 + blk
                        for q in range(2):
                            at, hp = 2 * blk + q, 2 * j + q
                            last = nc.tensor.matmul(bank[:, at * P:(at + 1) * P], keyT[r, hp, kc * P:(kc + 1) * P],
                                                    qryT[c][r, hp, :], start=(at == 2 - 2 * c), stop=True,
                                                    skip_group_check=True)
                    last.then_inc(bank_done, 1)

            def exponents(c, j):
                pe.wait_ge(soft_ready, NB * c + j + 1)
                for e in range(2):
                    bank, s = bank_of("z", c, j, e), notlog[:, e, :]
                    last = nc.tensor.matmul(bank[:, T:2 * T], later[:], s[:, T:2 * T], start=False, stop=True,
                                            skip_group_check=True)
                    if c:
                        nc.tensor.matmul(bank[:, 0:T], minus1[:], s[:, T:2 * T], start=False, stop=True,
                                         skip_group_check=True)
                        last = nc.tensor.matmul(bank[:, 0:T], later[:], s[:, 0:T], start=False, stop=True,
                                                skip_group_check=True)
                last.then_inc(expo_ready, 1)

            def heads_out(c, j):
                pe.wait_ge(weight_ready, NB * c + j + 1)
                bank = take("heads", c, j)
                for e in range(2):
                    for q in range(2):
                        for blk in range(1 - c, 2):
                            hd = 4 * j + 2 * q + e
                            last = nc.tensor.matmul(bank[e * DH:(e + 1) * DH, q * P:(q + 1) * P],
                                                    value[:, c - 1 + blk, hd * DH:(hd + 1) * DH],
                                                    soft[:, e, (2 * blk + q) * P:(2 * blk + q + 1) * P],
                                                    start=(q == 0 and blk == 1 - c), stop=(blk == 1),
                                                    skip_group_check=True)
                last.then_inc(bank_done, 1)

            def mixer_slot(c, t):
                if t == 0:
                    if c == 1:
                        for hd in (6, 7, 8):
                            if hd < HEADS:
                                query(1, 0, hd)
                            score(1, 0, hd - 1)
                    transpose_norm("kv", c)
                if t == 1:
                    wait_read(pe, "turn", "kv", c, 1)
                if t in (3, 5, 7, 9):
                    exponents(c, (t - 3) // 2)
                for name, j in PROJECTED.get(t, []):
                    if name == "z":
                        wait_read(pe, "qry", c, j)
                        logits(c, j)
                    elif name == "heads":
                        heads_out(c, j)
                    elif name == "val":
                        to_tokens(take(name, c, j)[:, 0:COLS], weights_of(name, c, j), kvT).then_inc(bank_done, 1)
                    else:
                        to_features(take(name, c, j), weights_of(name, c, j), kvT if name == "key" else mixT, P)
                if t == 7 and c == 0:
                    transpose_subkeys(1)
                if t == 10:
                    wait_read(pe, "heads", c, NB - 1)
                if t in (10, 11):
                    for q in (2 * (t - 10), 2 * (t - 10) + 1):
                        to_tokens(take("out", c, q)[:, 0:COLS], weights_of("out", c, q), headT[c]).then_inc(bank_done, 1)
                if t == 12:
                    transpose_norm("ffn1", c)
                    wait_read(pe, "turn", "ffn1", c, 1)
                    query(1, c, 0)
                for hd in {13: [1], 14: [2, 3], 15: [4, 5]}.get(t, []):
                    query(1, c, hd)
                    score(1, c, hd - 1)

            pe.wait_ge(consts, 10)
            transpose_subkeys(0)
            pe.wait_ge(vec_loaded, 48)
            bank = take("vectors")
            nc.tensor.transpose(bank[:, 0:48], vec_rows[:, :], ident[0:48, 0:48]).then_inc(bank_done, 1)

            for c in range(CH):
                transpose_norm("mix0", c)
            wait_read(pe, "turn", "mix0", CH - 1, 1)
            for j in range(NB):
                for part in (2, 1, 0):
                    to_features(take("conv", j, part), weights_of("conv", j, part), xT, T)
            wait_read(pe, "conv", NB - 1, 0)
            out_half(0, 0)
            out_half(0, 1)
            out_half(1, 0)

            for c in range(CH):
                transpose_norm("ffn0", c)
                wait_read(pe, "turn", "ffn0", c, 1)
                query(0, c, 0)
                score(0, c, 0)
                if c == 0:
                    out_half(1, 1)
            query(0, "both", 1)
            for hd in range(2, HEADS + 1):
                if hd < HEADS:
                    query(0, "both", hd)
                score(0, "both", hd - 1)

            combine_pair(0)
            with pe.Fori(1, HEADS // 2) as i:
                combine_pair(i)
            for c in range(CH):
                for t in range(SLOTS):
                    n = HEADS * (1 + c) + t // GROUPS
                    combine(n, n % 2, t % GROUPS)
                    mixer_slot(c, t)
            first = (STEPS - HEADS) // 2
            combine(2 * first, 0, 0)
            for hd in (6, 7, 8):
                if hd < HEADS:
                    query(1, 1, hd)
                score(1, 1, hd - 1)
            combine(2 * first, 0, 1)
            for g in range(GROUPS):
                combine(2 * first + 1, 1, g)
            with pe.Fori(first + 1, STEPS // 2) as i:
                combine_pair(i)
            assert taken[0] == len(fills)

        @block.scalar
        def _(act):
            act.dma_start(gain[:], norm_ffn[0].partition_broadcast(P)).then_inc(gain_loaded, 16)

            steps = [0]

            def own(ins):
                ins.then_inc(act_step, 1)
                steps[0] += 1
                act.wait_ge(act_step, steps[0])

            read_last = [-1]

            def read(name, dst, view=lambda bank: bank, scale=1.0):
                n = FILL[name]
                assert fills[n][0] == "act" and n > read_last[0], name
                read_last[0] = n
                act.wait_ge(bank_done, n + 1)
                nc.scalar.activation(dst, view(banks[:, fills[n][1], :]), ACT.Copy, scale=scale).then_inc(bank_read["act"], 1)

            def by_tokens(bank):
                return bank.rearrange("p (k t) -> p k t", t=P)

            def norm_sums(norm, c):
                wait_input(act, norm, c)
                nc.scalar.activation(xn[:, c, :], h[:, c, :], ACT.Square, accum_out=stat[:, 0, c:c + 1]).then_inc(squares, 1)
                act.wait_ge(means, normed_count(norm, c))
                own(nc.scalar.activation(stat[:, 2, c:c + 1], stat[:, 1, c:c + 1], ACT.Ln))
                nc.scalar.activation(stat[:, 3, c:c + 1], stat[:, 2, c:c + 1], ACT.Exp, scale=-0.5).then_inc(estimates, 1)

            def turned_subkeys(layer):
                for j in range(2 * HEADS // 4):
                    read(("subkeys", layer, j), subT[:, 4 * j:4 * j + 4, :], by_tokens)

            def turned_norm(norm, c, dst):
                for half in range(2):
                    read(("turn", norm, c, half), dst[:, 4 * half:4 * half + 4, :], by_tokens)

            def queries(layer, c, hd):
                tokens = T if c == "both" else P
                prev = ("score", layer, c if (layer or hd > 2) else 1, hd - 2)
                if hd >= 2:
                    wait_filled(act, *prev)
                elif hd == 0 and c == 1:
                    wait_filled(act, "score", layer, 0, 0 if layer == 0 else HEADS - 2)
                elif hd == 1 and c == 1:
                    wait_filled(act, "score", layer, 0, HEADS - 1)
                read(("query", layer, c, hd), queryT[:, hd % 2, :, 0:tokens],
                     lambda bank: bank[:, 0:2 * tokens].rearrange("p (s t) -> p s t", s=2))

            def scored(layer, c, hd):
                if c == "both":
                    read(("score", layer, c, hd), scores[:, hd:hd + HEADS + 1:HEADS, :],
                         lambda bank: bank.rearrange("p (c k) -> p c k", c=CH))
                else:
                    read(("score", layer, c, hd), scores[:, c * HEADS + hd, :], lambda bank: bank[:, 0:2 * KEYS])

            def gates(n, b):
                act.wait_ge(top_ready, n + 1)
                nc.scalar.activation(gate[b][:], top[b][:], ACT.Exp, bias=negmax[:, b:b + 1],
                                     accum_out=gate_sum[:, b:b + 1]).then_inc(gate_done, 1)

            def weigh(n, b, g):
                ks = slice(g * GROUP, (g + 1) * GROUP)
                act.wait_ge(dot_done, TOPK * n + GROUP * (g + 1))
                nc.scalar.activation(gelu[b][:, ks], dots[b][:, ks], ACT.Gelu).then_inc(gelu_done, 1)
                act.wait_ge(coef_ready, GROUPS * n + g + 1)
                for j in range(GROUP):
                    k = g * GROUP + j
                    if not (isinstance(n, int) and n == 0 and g == 0):
                        act.wait_ge(v_used, TOPK * n + k - GROUP + 1)
                    nc.scalar.activation(diag[:, j, :], ident[:], ACT.Copy, scale=coef[b][:, k:k + 1]).then_inc(diag_ready, 1)

            def weigh_pair(i, last=False):
                for b in range(2):
                    n = 2 * i + b
                    weigh(n, b, 0)
                    if not (last and b == 1):
                        gates(n + 1, 1 - b)
                    weigh(n, b, 1)

            def next_gain(norm, c, vector):
                act.wait_ge(normed, normed_count(norm, c))
                act.dma_start(gain[:], vector.partition_broadcast(P)).then_inc(gain_loaded, 16)

            def z_banks(c, j):
                return banks[:, 2:4, (1 - c) * T:]

            def logs(c, j):
                wait_filled(act, "z", c, j, 1)
                s = soft[:, :, (1 - c) * T:]
                nc.scalar.preload_act_table_set("natural_log_exp_and_others")
                own(nc.scalar.activation(s, z_banks(c, j), ACT.Abs))
                own(nc.scalar.activation(s, s, ACT.Exp, scale=-1.0))
                nc.scalar.activation(s, s, ACT.Ln, bias=1.0).then_inc(log_done, 1)

            def weights(c, j):
                wait_read(act, "z", c, j, 1)
                s = soft[:, :, (1 - c) * T:]
                nc.scalar.activation(s, s, ACT.Exp).then_inc(weight_ready, 1)

            def mixer_slot(c, t):
                if t in (0, 12):
                    nc.scalar.preload_act_table_set("natural_log_exp_and_others")
                    norm_sums("kv" if t == 0 else "ffn1", c)
                if t == 0 and c == 1:
                    for hd in (6, 7, 8):
                        if hd < HEADS:
                            queries(1, 0, hd)
                        scored(1, 0, hd - 1)
                for name, j in PROJECTED.get(t, []):
                    if name == "z":
                        logs(c, j)
                    elif name == "heads":
                        weights(c, j)
                        read(("heads", c, j), headT[c][:, 2 * j:2 * j + 2, :],
                             lambda bank: bank[:, 0:2 * P].rearrange("p (s t) -> p s t", s=2))
                    elif name == "val":
                        read((name, c, j), value[:, c, j * COLS:(j + 1) * COLS], lambda bank: bank[:, 0:COLS])
                    else:
                        dst = keyT[:, 2 * j:2 * j + 2, c * P:(c + 1) * P] if name == "key" else qryT[c][:, 2 * j:2 * j + 2, :]
                        read((name, c, j), dst, lambda bank: bank[:, 0:2 * P].rearrange("p (s t) -> p s t", s=2),
                             scale=1.0 if name == "key" else float(DH) ** -0.5)
                if t == 7 and c == 0:
                    turned_subkeys(1)
                if t == 12:
                    turned_norm("ffn1", c, kvT)
                    queries(1, c, 0)
                if t == 13 and c == 1:
                    next_gain("ffn1", 1, norm_final)
                for hd in {13: [1], 14: [2, 3], 15: [4, 5]}.get(t, []):
                    queries(1, c, hd)
                    scored(1, c, hd - 1)

            nc.scalar.preload_act_table_set("natural_log_exp_and_others")
            for c in range(CH):
                norm_sums("mix0", c)
            act.wait_ge(consts, 10)
            turned_subkeys(0)
            read(("vectors",), vecs[:, :], lambda bank: bank[:, 0:48])
            for j in range(NB):
                if j >= 2:
                    wait_read(act, "conv", j - 2, 1)
                read(("conv", j, 2), conv_h[:, j % 2], lambda bank: bank.rearrange("p (s t) -> p s t", s=2))
            for c in range(CH):
                norm_sums("ffn0", c)
                turned_norm("ffn0", c, xT[:, :, c * P:(c + 1) * P])
                queries(0, c, 0)
                scored(0, c, 0)
            queries(0, "both", 1)
            for hd in range(2, HEADS + 1):
                if hd < HEADS:
                    queries(0, "both", hd)
                scored(0, "both", hd - 1)
            next_gain("ffn0", CH - 1, norm_ffn[1])

            gates(0, 0)
            weigh_pair(0)
            with act.Fori(1, HEADS // 2) as i:
                weigh_pair(i)
            for c in range(CH):
                for t in range(SLOTS):
                    n = HEADS * (1 + c) + t // GROUPS
                    weigh(n, n % 2, t % GROUPS)
                    if t == SLOTS - 1 or (t % GROUPS == 0 and t < SLOTS - GROUPS):
                        gates(n + 1, 1 - n % 2)
                    mixer_slot(c, t)
            first = (STEPS - HEADS) // 2
            weigh(2 * first, 0, 0)
            gates(2 * first + 1, 1)
            nc.scalar.preload_act_table_set("natural_log_exp_and_others")
            norm_sums("final", 0)
            for hd in (6, 7, 8):
                if hd < HEADS:
                    queries(1, 1, hd)
                scored(1, 1, hd - 1)
            weigh(2 * first, 0, 1)
            weigh(2 * first + 1, 1, 0)
            gates(2 * first + 2, 0)
            weigh(2 * first + 1, 1, 1)
            with act.Fori(first + 1, STEPS // 2 - 1) as i:
                weigh_pair(i)
            weigh_pair(STEPS // 2 - 1, last=True)
            nc.scalar.preload_act_table_set("natural_log_exp_and_others")
            norm_sums("final", 1)

        @block.vector
        def _(dve):
            done = [0]

            def mark(ins):
                ins.then_inc(dve_step, 1)
                done[0] = done[0] + 1
                return done[0]

            def need(value):
                dve.wait_ge(dve_step, value)

            def need_apart(value):
                need(value)
                if not isinstance(value, int):
                    dve.sem_inc(search_clear, 1)

            def norm_stream(norm, c):
                mean, y, r, t = (stat[:, q, c:c + 1] for q in (1, 3, 4, 5))
                dve.wait_ge(squares, normed_count(norm, c))
                nc.vector.tensor_scalar(mean, stat[:, 0, c:c + 1], 1.0 / D, EPS, ALU.mult, ALU.add).then_inc(means, 1)
                dve.wait_ge(estimates, normed_count(norm, c))
                need(mark(nc.vector.tensor_tensor(t, y, y, ALU.mult)))
                need(mark(nc.vector.tensor_tensor(t, t, mean, ALU.mult)))
                need(mark(nc.vector.tensor_scalar(t, t, -0.5, 1.5, ALU.mult, ALU.add)))
                need(mark(nc.vector.tensor_tensor(r, y, t, ALU.mult)))
                if norm in ("mix0", "kv"):
                    nc.vector.tensor_scalar(xn[:, c, :], h[:, c, :], r, None, ALU.mult).then_inc(normed, 1)
                else:
                    dve.wait_ge(gain_loaded, 16 * (1 + ["ffn0", "ffn1", "final"].index(norm)))
                    nc.vector.scalar_tensor_tensor(out=xn[:, c, :], in0=h[:, c, :], scalar=r, in1=gain[:],
                                                   op0=ALU.mult, op1=ALU.mult).then_inc(normed, 1)

            def turned_norm(norm, c, outs):
                for half in range(2):
                    wait_filled(dve, "turn", norm, c, half)
                    for t, (dst, col) in enumerate(outs):
                        g = vecs[:, col + 4 * half:col + 4 * half + 4].unsqueeze(2).to_broadcast([P, 4, P])
                        ins = nc.vector.tensor_tensor(dst[:, 4 * half:4 * half + 4, :],
                                                      bank_of("turn", norm, c, half).rearrange("p (k t) -> p k t", t=P), g, ALU.mult)
                    ins.then_inc(bank_read["dve"], 1)

            def add_mixer(c):
                for half in range(2):
                    dve.wait_ge(out_done, 2 * c + half + 1)
                    at = h[:, c, half * 512:(half + 1) * 512]
                    nc.vector.tensor_tensor(at, sums[:, 2 * c + half, :], at, ALU.add).then_inc(out_added, 1)

            def top16(values, indices, src, scratch, start):
                need_apart(start)
                a = mark(nc.vector.max(values[:, 0:8], src))
                need_apart(a)
                r = mark(nc.vector.match_replace(scratch, values[:, 0:8], src, FOUND))
                mark(nc.vector.max_index(indices[:, 0:8], values[:, 0:8], src))
                need_apart(r)
                b = mark(nc.vector.max(values[:, 8:16], scratch))
                need_apart(b)
                return mark(nc.vector.max_index(indices[:, 8:16], values[:, 8:16], scratch))

            def find_experts(n, at, b, layer):
                s = mark(nc.vector.tensor_copy(srch, scores[:, bass.ds(at, 1), :].rearrange("p a k -> p (a k)")))
                for p in range(2):
                    e = top16(side_v[:, p, :], side_i[:, p, :], srch[:, p * KEYS:(p + 1) * KEYS],
                              srch2[:, p * KEYS:(p + 1) * KEYS], s)
                need(e)
                c = mark(nc.vector.tensor_tensor(cand.rearrange("p (a b) -> p a b", b=TOPK),
                                                 side_v[:, 0, :].unsqueeze(2).to_broadcast([P, TOPK, TOPK]),
                                                 side_v[:, 1, :].unsqueeze(1).to_broadcast([P, TOPK, TOPK]), ALU.add))
                e = top16(top[b][:], cand_i[:], cand, cand2, c)
                need(e)
                nc.vector.tensor_scalar(negmax[:, b:b + 1], top[b][:, 0:1], -1.0, None, ALU.mult).then_inc(top_ready, 1)
                mark(nc.vector.tensor_scalar(digit[:, 0, :], cand_i[:], 4, None, ALU.logical_shift_right))
                d = mark(nc.vector.tensor_scalar(digit[:, 1, :], cand_i[:], TOPK - 1, None, ALU.bitwise_and))
                need(d)
                d = mark(nc.vector.tensor_tensor(pick.rearrange("p a k j -> p (a k) j"),
                                                 digit[:].rearrange("p a k -> p (a k)").unsqueeze(2).to_broadcast([P, 2 * TOPK, TOPK]),
                                                 iota[:].unsqueeze(1).to_broadcast([P, 2 * TOPK, TOPK]), ALU.is_equal))
                need(d)
                d = mark(nc.vector.tensor_tensor(pick, pick,
                                                 side_i[:].unsqueeze(2).to_broadcast([P, 2, TOPK, TOPK]), ALU.mult))
                need(d)
                d = mark(nc.vector.tensor_reduce(picked[:].rearrange("p a k -> p (a k)"),
                                                 pick.rearrange("p a k j -> p (a k) j"), AX_X, ALU.add))
                need(d)
                d = mark(nc.vector.scalar_tensor_tensor(out=expert_f[:], in0=picked[:, 0, :], scalar=float(KEYS),
                                                        in1=picked[:, 1, :], op0=ALU.mult, op1=ALU.add))
                need(d)
                nc.vector.tensor_scalar(expert[b][:], expert_f[:], float(layer * EXPERTS), None, ALU.add).then_inc(expert_ready, 1)

            def dot_group(n, chunk, b, g):
                for j in range(GROUP):
                    k = g * GROUP + j
                    dve.wait_ge(u_landed[j], 16 * (GROUPS * n + g + 1))
                    nc.vector.scalar_tensor_tensor(out=u_row[j], in0=u_row[j], scalar=1.0,
                                                   in1=xn[:, bass.ds(chunk, 1), :].rearrange("p c d -> p (c d)"),
                                                   op0=ALU.mult, op1=ALU.mult,
                                                   accum_out=dots[b][:, k:k + 1]).then_inc(dot_done, 1)

            def add_head(n, chunk, b):
                dve.wait_ge(v_used, TOPK * (n + 1))
                at = h[:, bass.ds(chunk, 1), :].rearrange("p c d -> p (c d)")
                nc.vector.tensor_tensor(at, sums[:, 2 * b:2 * b + 2, :].rearrange("p a d -> p (a d)"), at,
                                        ALU.add).then_inc(head_added, 1)

            def coefficients(n, b, g):
                dve.wait_ge(gelu_done, GROUPS * n + g + 1)
                if g == 0:
                    dve.wait_ge(gate_done, n + 1)
                    need(mark(nc.vector.reciprocal(gate_inv[:, b:b + 1], gate_sum[:, b:b + 1])))
                ks = slice(g * GROUP, (g + 1) * GROUP)
                nc.vector.scalar_tensor_tensor(out=coef[b][:, ks], in0=gelu[b][:, ks], scalar=gate_inv[:, b:b + 1],
                                               in1=gate[b][:, ks], op0=ALU.mult, op1=ALU.mult).then_inc(coef_ready, 1)

            def step(n, b, chunk, before, at, layer, look=True):
                dot_group(n, chunk, b, 0)
                if not (isinstance(n, int) and n == 0):
                    add_head(n - 1, before, 1 - b)
                if look:
                    find_experts(n + 1, at, 1 - b, layer)
                coefficients(n, b, 0)

            def second_group(n, b, chunk):
                dot_group(n, chunk, b, 1)
                coefficients(n, b, 1)

            def expert_pair(i, chunk, layer, last=False):
                for b in range(2):
                    n = 2 * i + b
                    step(n, b, chunk, chunk, n + 1 - NH * layer, layer, look=not (last and b == 1))
                    second_group(n, b, chunk)

            def looped_pairs(first, end, per, chunk, layer):
                start = done[0]
                with dve.Fori(first, end) as i:
                    done[0] = start - per * first + per * i
                    expert_pair(i, chunk, layer)
                done[0] = start + per * (end - first)

            def z_banks(c, j):
                return banks[:, 2:4, (1 - c) * T:]

            def softplus(c, j):
                dve.wait_ge(log_done, NB * c + j + 1)
                s = notlog[:, :, (1 - c) * T:]
                need(mark(nc.vector.scalar_tensor_tensor(out=s, in0=z_banks(c, j), scalar=0.0, in1=soft[:, :, (1 - c) * T:],
                                                         op0=ALU.max, op1=ALU.add)))
                d = notlog[:, :, T:].rearrange("p e (q t) -> p e q t", t=P)
                nc.vector.tensor_tensor(d, d, keep[:].unsqueeze(1).unsqueeze(1).to_broadcast([P, 2, 2, P]),
                                        ALU.mult).then_inc(soft_ready, 1)

            def exponent(c, j):
                dve.wait_ge(expo_ready, NB * c + j + 1)
                if c:
                    nc.vector.tensor_scalar(soft[:, :, 0:T], banks[:, 2:4, 0:T], 0.0, None, ALU.min)
                for e in range(2):
                    nc.vector.scalar_tensor_tensor(out=soft[:, e, T:].rearrange("p (q t) -> p q t", t=P),
                                                   in0=bank_of("z", c, j, e)[:, T:].rearrange("p (q t) -> p q t", t=P),
                                                   scalar=0.0, in1=hide[:].unsqueeze(1).to_broadcast([P, 2, P]),
                                                   op0=ALU.min, op1=ALU.add).then_inc(bank_read["dve"], 1)

            def mixer_slot(c, t):
                if t == 0:
                    norm_stream("kv", c)
                if t == 1:
                    turned_norm("kv", c, [(kvT, 2 * KT), (mixT, KT)])
                if t in (3, 5, 7, 9):
                    softplus(c, (t - 3) // 2)
                if t in (4, 6, 8, 10):
                    exponent(c, (t - 4) // 2)
                if t == 12:
                    for q in range(NB):
                        wait_filled(dve, "out", c, q)
                        at = h[:, c, q * COLS:(q + 1) * COLS]
                        nc.vector.tensor_tensor(at, bank_of("out", c, q)[:, 0:COLS], at, ALU.add).then_inc(bank_read["dve"], 1)
                    norm_stream("ffn1", c)

            for b in range(2):
                mark(nc.vector.memset(conv_u[:, b, :, 0:TAPS - 1], 0.0))
            for c in range(CH):
                norm_stream("mix0", c)
            wait_read(dve, "vectors")
            for c in range(CH):
                turned_norm("mix0", c, [(xT[:, :, c * P:(c + 1) * P], 0)])
            for j in range(NB):
                u, y = conv_u[:, j % 2], conv_y[:, j % 2]
                c_bank, b_bank = (bank_of("conv", j, part).rearrange("p (s t) -> p s t", s=2) for part in (1, 0))
                wait_read(dve, "conv", j, 2)
                wait_filled(dve, "conv", j, 1)
                nc.vector.tensor_tensor(u[:, :, TAPS - 1:], c_bank, conv_h[:, j % 2], ALU.mult).then_inc(bank_read["dve"], 1)
                wait_read(dve, "conv", j, 1)
                tap = lambda i, s: vecs[:, (3 + i) * KT + 2 * j + s:(3 + i) * KT + 2 * j + s + 1]
                for i in range(TAPS):
                    for s in range(2):
                        src = u[:, s, i:i + T]
                        if i == 0:
                            e = mark(nc.vector.tensor_scalar(y[:, s, :], src, tap(i, s), None, ALU.mult))
                        else:
                            need(e_of[s])
                            e = mark(nc.vector.scalar_tensor_tensor(out=y[:, s, :], in0=src, scalar=tap(i, s), in1=y[:, s, :],
                                                                    op0=ALU.mult, op1=ALU.add))
                        if i == 0 and s == 0:
                            e_of = [0, 0]
                        e_of[s] = e
                need(e)
                wait_filled(dve, "conv", j, 0)
                nc.vector.tensor_tensor(gatedT[:, 2 * j:2 * j + 2, :], b_bank, y, ALU.mult).then_inc(bank_read["dve"], 1)
            for c in range(CH):
                add_mixer(c)
                norm_stream("ffn0", c)
                if c == 0:
                    wait_read(dve, "score", 0, 0, 0)
                    find_experts(0, 0, 0, 0)

            before = done[0]
            for b in range(2):
                if b == 0:
                    dot_group(0, 0, 0, 0)
                    wait_read(dve, "score", 0, "both", 1)
                    find_experts(1, 1, 1, 0)
                    coefficients(0, 0, 0)
                else:
                    wait_read(dve, "score", 0, "both", 2)
                    step(1, 1, 0, 0, 2, 0)
                second_group(b, b, 0)
            per = done[0] - before
            wait_read(dve, "score", 0, "both", HEADS - 1)
            looped_pairs(1, HEADS // 2, per, 0, 0)

            for c in range(CH):
                chunk = 1 - c
                for t in range(SLOTS):
                    hd = t // GROUPS
                    n = HEADS * (1 + c) + hd
                    b = n % 2
                    if t % GROUPS == 0:
                        if c == 1 and hd + 1 < HEADS:
                            wait_read(dve, "score", 1, 0, hd + 1)
                        step(n, b, chunk, chunk if hd else c, n + 1 - NH * c, c, look=hd + 1 < HEADS)
                    else:
                        second_group(n, b, chunk)
                    if t == SLOTS - 1:
                        wait_read(dve, "score", 1, c, 0)
                        find_experts(n + 1, n + 1 - NH, 1 - b, 1)
                    mixer_slot(c, t)

            first = (STEPS - HEADS) // 2
            wait_read(dve, "score", 1, 1, 1)
            step(2 * first, 0, 1, 0, HEADS + 1, 1)
            norm_stream("final", 0)
            second_group(2 * first, 0, 1)
            wait_read(dve, "score", 1, 1, 2)
            step(2 * first + 1, 1, 1, 1, HEADS + 2, 1)
            second_group(2 * first + 1, 1, 1)
            wait_read(dve, "score", 1, 1, HEADS - 1)
            looped_pairs(first + 1, STEPS // 2 - 1, per, 1, 1)
            expert_pair(STEPS // 2 - 1, 1, 1, last=True)
            add_head(STEPS - 1, 1, 1)
            norm_stream("final", 1)


_INS = ["x", "norm_mix", "norm_ffn", "conv_w_in", "conv_kernel", "conv_w_out", "norm_kv", "w_kv", "attn_w_q",
        "attn_w_o", "peer_w_query", "peer_subkeys", "peer_u", "peer_v", "norm_final"]


def kernel(**inputs):
    import numpy as _np
    import concourse.bacc as _bacc
    from concourse import mybir as _mybir
    from concourse.bass_utils import run_bass_kernel_spmd as _run

    nc = _bacc.Bacc("TRN2", target_bir_lowering=False, num_devices=1)
    arrays, args = {}, []
    for name in _INS:
        a = _np.ascontiguousarray(inputs[name])
        arrays[f"in_{name}"] = a
        args.append(nc.dram_tensor(f"in_{name}", a.shape, _mybir.dt.from_np(a.dtype), kind="ExternalInput").ap())
    shape = inputs["x"].shape
    args.append(nc.dram_tensor("out_stream", shape, _mybir.dt.float32, kind="ExternalOutput").ap())
    trunk(nc, *args)
    r = _run(nc, [arrays], core_ids=[0])
    return r.results[0]["out_stream"]
```

```python
from contextlib import ExitStack

import concourse.bass as bass
from concourse import mybir

F32 = mybir.dt.float32
U32 = mybir.dt.uint32
ALU = mybir.AluOpType
ACT = mybir.ActivationFunctionType
AX_X = mybir.AxisListType.X

P = 128
EPS = 1e-6
FOUND = -3.0e38
MASKED = -1.0e4
COLS = 256
W_RING = 3
W_KEPT = 4
U_SLOTS = 8
V_SLOTS = 8
GROUP = 8


def trunk(nc, x, norm_mix, norm_ffn, conv_w_in, conv_kernel, conv_w_out, norm_kv, w_kv,
          attn_w_q, attn_w_o, peer_w_query, peer_subkeys, peer_u, peer_v, norm_final, out):
    _, T, D = x.shape
    LAYERS, HEADS, _, KEYS, KD = peer_subkeys.shape
    EXPERTS = peer_u.shape[1]
    TAPS = conv_kernel.shape[1]
    CH = T // P
    KT = D // P
    TOPK = 16
    DH = 64
    PAIRS = D // (2 * DH)
    NH = CH * HEADS
    STEPS = LAYERS * NH
    GROUPS = TOPK // GROUP
    assert (CH, KEYS, KD, COLS) == (2, P, P, 2 * P) and GROUPS == 2 and D == PAIRS * P and KT == PAIRS
    W_EARLY = (U_SLOTS + V_SLOTS) // 2
    assert U_SLOTS == GROUP and V_SLOTS == GROUP and TAPS == 3 and LAYERS == 2

    NB = D // COLS
    SLOTS = HEADS * GROUPS
    fills, FILL = [], {}
    turn = {"block": [0, 1], "side": [2, 3]}

    def fill(by, bank, *name):
        if bank in turn:
            turn[bank].reverse()
            bank = turn[bank][1]
        FILL[name] = len(fills)
        fills.append((by, bank))

    fill("act", "side", "vectors")
    for c in range(CH):
        for half in range(2):
            fill("dve", "side", "turn", "mix0", c, half)
    PARTS = ((2, "act"), (1, "dve"), (0, "dve"))
    BOTH = 1

    def fills_of_conv(c, j):
        for part, by in PARTS:
            fill(by, "block", "conv", c, j, part)

    def fills_of_query(layer, c, hd):
        fill("act", "block", "query", layer, c, hd)
        fill("act", "side", "score", layer, c, hd)

    FIRST = 3
    for j in range(NB):
        fills_of_conv("both" if j < BOTH else 0, j)
    for q in range(2 * HEADS // 4):
        fill("act", (2, 3, 0, 1)[q], "subkeys", 0, q)
    for half in range(2):
        fill("act", 2 + half, "turn", "ffn0", 0, half)
    fills_of_query(0, 0, 0)
    for j in range(BOTH, NB):
        fills_of_conv(1, j)
    fills_of_query(0, 0, 1)
    QUERIED = {1: [(0, 2)], 2: [(1, hd) for hd in range(FIRST)]}
    QUERIED.update({hd: [("both", hd)] for hd in range(FIRST, HEADS)})
    for t in QUERIED:
        if t == 2:
            for half in range(2):
                fill("act", "side", "turn", "ffn0", 1, half)
        for c, hd in QUERIED[t]:
            fills_of_query(0, c, hd)

    def fills_of_heads(c, hd):
        if hd < HEADS:
            fill("act", "block", "query", 1, c, hd)
        fill("act", "side", "score", 1, c, hd - 1)

    def fills_of_slot(c, t):
        for name, j in PROJECTED.get(t, []):
            if name in ("z", "heads"):
                if name == "z":
                    for e in range(2):
                        fill("dve", 2 + e, "z", c, j, e)
                else:
                    fill("act", "block", "heads", c, j)
            else:
                fill("act", "block", name, c, j)

    PROJECTED = {1: [("key", 0), ("qry", 0), ("val", 0)], 2: [("z", 0), ("key", 1), ("qry", 1)],
                 3: [("val", 1), ("key", 2)], 4: [("heads", 0), ("z", 1), ("qry", 2), ("val", 2)],
                 5: [("key", 3), ("qry", 3)], 6: [("heads", 1), ("z", 2), ("val", 3)],
                 8: [("heads", 2), ("z", 3)], 10: [("heads", 3)]}
    assert NB == 4 and SLOTS == 16 and HEADS == 8
    for c in range(CH):
        for t in range(SLOTS + 1):
            if t == SLOTS and c == 0:
                continue
            if t in (0, SLOTS) and (c == 1):
                for hd in (6, 7, 8):
                    fills_of_heads(0 if t == 0 else 1, hd)
            if t == 0:
                for half in range(2):
                    fill("dve", "side", "turn", "kv", c, half)
            fills_of_slot(c, t)
            if t == 7 and c == 0:
                for q in range(2 * HEADS // 4):
                    fill("act", "block", "subkeys", 1, q)
            if t in (10, 11):
                for q in (0, 1):
                    fill("dve", 2 * (t - 10) + q, "out", c, 2 * (t - 10) + q)
            if t == 12:
                for half in range(2):
                    fill("act", "side", "turn", "ffn1", c, half)
                fill("act", "block", "query", 1, c, 0)
            if t in (13, 14, 15):
                for hd in {13: [1], 14: [2, 3], 15: [4, 5]}[t]:
                    fills_of_heads(c, hd)

    def nth(n):
        by = fills[n][0]
        return sum(f[0] == by for f in fills[:n + 1])

    blocks, BLOCK, freed_by = [], {}, []

    def stream(w, col, freed, *name):
        BLOCK[name] = len(blocks)
        blocks.append((w, col))
        freed_by.append(freed)

    for j in range(NB):
        for part, _ in PARTS:
            stream(conv_w_in[0], part * D + j * COLS, FILL["conv", "both" if j < BOTH else 1, j, part], "conv", j, part)
        if j == 1:
            stream(peer_subkeys[0], None, FILL["subkeys", 0, 3], "subkeys", 0)
    for q in range(NB):
        stream(conv_w_out[0], q * COLS, ("half", q // 2), "out0", q)
    for hd in range(HEADS):
        stream(peer_w_query[0], hd * COLS, FILL["query", 0, "both" if hd >= FIRST else 1, hd], "query", 0, hd)
    for c in range(CH):
        for t in sorted(PROJECTED):
            for name, j in PROJECTED[t]:
                if name in ("key", "qry", "val"):
                    w, first = {"key": (w_kv, 0), "qry": (attn_w_q[0], 0), "val": (w_kv, D)}[name]
                    stream(w, first + j * COLS, FILL[name, c, j], name, c, j)
            if t == 6 and c == 0:
                stream(peer_subkeys[1], None, FILL["subkeys", 1, 3], "subkeys", 1)
        for q in range(NB if c == 0 else 0):
            stream(attn_w_o[0], q * COLS, FILL["out", 1, q], "out", q)
        for hd in range(HEADS):
            stream(peer_w_query[1], hd * COLS, FILL["query", 1, c, hd], "query", 1 + c, hd)
    KEPT = W_RING + W_EARLY
    EARLY_SLOTS = [0, 1, 2, 3, 4, 5, 6, 7, 8, 9, 10, 1, 2, 11, 12, 13, 14, 15]
    assert len(EARLY_SLOTS) == BLOCK["query", 0, 0] + 1 and W_RING == 3 and KEPT == 11
    w_slot, ringed = list(EARLY_SLOTS), 0
    for m in range(len(EARLY_SLOTS), len(blocks)):
        kept = m - BLOCK["out", 0]
        w_slot.append(KEPT + kept if 0 <= kept < W_KEPT else ringed % W_RING)
        ringed += not 0 <= kept < W_KEPT

    def before_in_slot(m):
        earlier = [b for b in range(m) if w_slot[b] == w_slot[m]]
        return (earlier[-1] if earlier else None), len(earlier)

    NORM_ORDER = [("mix0", 0), ("mix0", 1), ("ffn0", 0), ("ffn0", 1), ("kv", 0), ("ffn1", 0), ("kv", 1), ("ffn1", 1),
                  ("final", 0), ("final", 1)]

    with ExitStack() as ctx:
        def sb(name, shape, dt=F32):
            return ctx.enter_context(nc.sbuf_tensor(name, shape, dt))

        def sem(name):
            return ctx.enter_context(nc.semaphore(name))

        ident = sb("ident", [P, P])
        keep = sb("keep", [P, P])
        hide = sb("hide", [P, P])
        later = sb("later", [P, P])
        minus1 = sb("minus1", [P, P])
        iota = sb("iota", [P, TOPK], U32)
        vec_rows = sb("vec_rows", [48, P])
        vecs = sb("vecs", [P, 48])
        gain = sb("gain", [P, D])
        h = sb("h", [P, CH, D])
        xn = sb("xn", [P, CH, D])
        xT = sb("xT", [P, KT, T])
        stat = sb("stat", [P, 6, CH])
        wring = sb("wring", [P, W_RING, KT, COLS])
        wkept = sb("wkept", [P, W_KEPT, KT, COLS])
        subT = sb("subT", [P, 2 * HEADS, KEYS])
        scores = sb("scores", [P, NH, 2 * KEYS])
        find = sb("find", [P, 4 * KEYS])
        srch = cand = find[:, 0:2 * KEYS]
        srch2 = cand2 = find[:, 2 * KEYS:4 * KEYS]
        pick = find[:, :].rearrange("p (a k j) -> p a k j", a=2, j=TOPK)
        side_v = sb("side_v", [P, 2, TOPK])
        side_i = sb("side_i", [P, 2, TOPK], U32)
        cand_i = sb("cand_i", [P, TOPK], U32)
        digit = sb("digit", [P, 2, TOPK], U32)
        picked = sb("picked", [P, 2, TOPK])
        expert_f = sb("expert_f", [P, TOPK])
        expert = [sb(f"expert{b}", [P, TOPK], U32) for b in range(2)]
        top = [sb(f"top{b}", [P, TOPK]) for b in range(2)]
        negmax = sb("negmax", [P, 2])
        gate = [sb(f"gate{b}", [P, TOPK]) for b in range(2)]
        gate_sum = sb("gate_sum", [P, 2])
        gate_inv = sb("gate_inv", [P, 2])
        dots = [sb(f"dots{b}", [P, TOPK]) for b in range(2)]
        gelu = [sb(f"gelu{b}", [P, TOPK]) for b in range(2)]
        coef = [sb(f"coef{b}", [P, TOPK]) for b in range(2)]
        diag = sb("diag", [P, GROUP, P])
        keyT = sb("keyT", [P, KT, T])
        value = sb("value", [P, CH, D])
        soft = sb("soft", [P, 2, 4 * P])
        spare = sb("spare", [P, 4 * (T + TAPS - 1)])
        notlog = spare[:, 0:8 * P].rearrange("p (e k) -> p e k", e=2)
        queryT = soft[:, :, :].rearrange("p b (s t) -> p b s t", t=T)
        kvT, mixT = xT[:, :, 0:P], xT[:, :, P:T]

        def work(c, part):
            a = scores[:, c * HEADS + part * HEADS // 2:c * HEADS + (part + 1) * HEADS // 2, :]
            return a.rearrange("p a k -> p (a k)").rearrange("p (k t) -> p k t", t=P)

        qryT = [work(c, 0) for c in range(CH)]
        headT = [work(c, 1) for c in range(CH)]
        rows = sb("rows", [P, U_SLOTS + V_SLOTS, D])
        u_row = [rows[:, j, :] for j in range(U_SLOTS)]
        v_row = [rows[:, U_SLOTS + j, :] for j in range(V_SLOTS)]
        flat = rows[:, :, :].rearrange("p s d -> p (s d)")
        w_place = [wring[:, j] for j in range(W_RING)] + [
            flat[:, j * KT * COLS:(j + 1) * KT * COLS].rearrange("p (k n) -> p k n", n=COLS) for j in range(W_EARLY)]
        assert W_EARLY * KT * COLS == (U_SLOTS + V_SLOTS) * D
        w_place += [wkept[:, j] for j in range(W_KEPT)]
        w_place.append(scores[:, HEADS:, :].rearrange("p a k -> p (a k)").rearrange("p (k n) -> p k n", n=COLS))

        by_group = lambda a: a.rearrange("p (g s t) -> p g s t", g=2, s=2)
        conv_h = by_group(keyT[:, 0:KT // 2, :].rearrange("p k t -> p (k t)"))
        conv_y = by_group(keyT[:, KT // 2:, :].rearrange("p k t -> p (k t)"))
        conv_u = by_group(spare[:, :])
        conv_halo = sb("conv_halo", [P, NB, 2, TAPS - 1])
        gatedT = value[:, :, :].rearrange("p c (k t) -> p (c k) t", t=T)

        sums = ctx.enter_context(nc.psum_tensor("sums", [P, 4, 512], F32))
        banks = ctx.enter_context(nc.psum_tensor("banks", [P, 4, 512], F32))

        def bank_of(*name):
            return banks[:, fills[FILL[name]][1], :]

        x_loaded = [sem(f"x_loaded{c}") for c in range(CH)]
        vec_loaded, gain_loaded = map(sem, ("vec_loaded", "gain_loaded"))
        consts = sem("consts")
        w_landed = [sem(f"w_landed{j}") for j in range(len(w_place))]
        u_landed = [sem(f"u_landed{j}") for j in range(U_SLOTS)]
        v_landed = [sem(f"v_landed{j}") for j in range(V_SLOTS)]
        bank_done = sem("bank_done")
        bank_read = {"act": sem("bank_read_by_act"), "dve": sem("bank_read_by_dve")}
        dve_step = sem("dve_step")
        act_step = sem("act_step")
        squares = sem("squares")
        means = sem("means")
        estimates = sem("estimates")
        normed = sem("normed")
        expert_ready = sem("expert_ready")
        top_ready = sem("top_ready")
        gate_done = sem("gate_done")
        slot_clear = sem("slot_clear")
        search_clear = sem("search_clear")
        dot_done = sem("dot_done")
        gelu_done = sem("gelu_done")
        coef_ready = sem("coef_ready")
        diag_ready = sem("diag_ready")
        v_used = sem("v_used")
        head_added = sem("head_added")
        out_done = sem("out_done")
        out_added = sem("out_added")
        log_done = sem("log_done")
        soft_ready = sem("soft_ready")
        expo_ready = sem("expo_ready")
        weight_ready = sem("weight_ready")
        stored = sem("stored")

        block = ctx.enter_context(nc.Block())

        def wait_filled(eng, *name):
            eng.wait_ge(bank_done, FILL[name] + 1)

        def wait_read(eng, *name):
            n = FILL[name]
            eng.wait_ge(bank_read[fills[n][0]], nth(n))

        def wait_input(eng, norm, c):
            if norm == "mix0":
                eng.wait_ge(x_loaded[c], 16)
            elif norm == "ffn0":
                eng.wait_ge(out_added, 2 * (c + 1))
            elif norm == "ffn1":
                wait_read(eng, "out", c, NB - 1)
            else:
                eng.wait_ge(head_added, NH * (norm == "final") + HEADS * (c + 1))

        def wait_freed(eng, m):
            if isinstance(freed_by[m], tuple):
                eng.wait_ge(out_done, 2 * (CH - 1) + freed_by[m][1] + 1)
            else:
                eng.wait_ge(bank_done, freed_by[m] + 1)

        def normed_count(norm, c):
            return NORM_ORDER.index((norm, c)) + 1

        @block.sync
        def _(sp):
            for c in range(CH):
                sp.dma_start(h[:, c, :], x[0, c * P:(c + 1) * P, :]).then_inc(x_loaded[c], 16)
            sp.dma_start(vec_rows[0:2 * KT, :], norm_mix.rearrange("l (k p) -> (l k) p", p=P)).then_inc(vec_loaded, 16)
            sp.dma_start(vec_rows[2 * KT:3 * KT, :], norm_kv.rearrange("(k p) -> k p", p=P)).then_inc(vec_loaded, 16)
            sp.dma_start(vec_rows[3 * KT:6 * KT, :], conv_kernel[0].rearrange("t (k p) -> (t k) p", p=P)).then_inc(vec_loaded, 16)
            for m, (w, col) in enumerate(blocks):
                before, _ = before_in_slot(m)
                if before is not None:
                    wait_freed(sp, before)
                at = w_place[w_slot[m]]
                if col is None:
                    sp.dma_start(at.rearrange("p k n -> p (k n)").rearrange("p (k n) -> p k n", n=KD),
                                 w.rearrange("h s n d -> n (h s) d")).then_inc(w_landed[w_slot[m]], 16)
                else:
                    sp.dma_start(at, w.rearrange("(k p) n -> p k n", p=P)[:, :, col:col + COLS]).then_inc(w_landed[w_slot[m]], 16)
            for c in range(CH):
                sp.wait_ge(normed, normed_count("final", c))
                sp.dma_start(out[0, c * P:(c + 1) * P, :], xn[:, c, :]).then_inc(stored, 16)
            sp.wait_ge(stored, 16 * CH)

        @block.gpsimd
        def _(pool):
            nc.gpsimd.memset(ident[:], 0.0).then_inc(consts, 1)
            nc.gpsimd.memset(keep[:], 1.0).then_inc(consts, 1)
            nc.gpsimd.memset(hide[:], 0.0).then_inc(consts, 1)
            nc.gpsimd.memset(later[:], -1.0).then_inc(consts, 1)
            nc.gpsimd.memset(minus1[:], -1.0).then_inc(consts, 1)
            nc.gpsimd.iota(iota[:], pattern=[[1, TOPK]], base=0, channel_multiplier=0).then_inc(consts, 1)
            pool.wait_ge(consts, 6)
            nc.gpsimd.affine_select(out=ident[:], in_=ident[:], compare_op=ALU.not_equal, fill=1.0, base=0,
                                    pattern=[[-1, P]], channel_multiplier=1).then_inc(consts, 1)
            nc.gpsimd.affine_select(out=keep[:], in_=keep[:], compare_op=ALU.is_gt, fill=0.0, base=0,
                                    pattern=[[1, P]], channel_multiplier=-1).then_inc(consts, 1)
            nc.gpsimd.affine_select(out=hide[:], in_=hide[:], compare_op=ALU.is_gt, fill=MASKED, base=0,
                                    pattern=[[1, P]], channel_multiplier=-1).then_inc(consts, 1)
            nc.gpsimd.affine_select(out=later[:], in_=later[:], compare_op=ALU.is_ge, fill=0.0, base=0,
                                    pattern=[[-1, P]], channel_multiplier=1).then_inc(consts, 1)

            u_table = peer_u.rearrange("l e d -> (l e) d")
            v_table = peer_v.rearrange("l e d -> (l e) d")

            def early_weights_used(row):
                slot = W_RING + row // 2
                wait_freed(pool, max(m for m in range(len(blocks)) if w_slot[m] == slot))
                pool.sem_inc(slot_clear, 1)

            def gather_pair(i):
                for b in range(2):
                    n = 2 * i + b
                    pool.wait_ge(expert_ready, n + 1)
                    pool.sem_inc(slot_clear, 1)
                    for g in range(GROUPS):
                        for j in range(GROUP):
                            if not (isinstance(n, int) and n == 0 and g == 0):
                                pool.wait_ge(dot_done, GROUP * (GROUPS * n + g - 1) + j + 1)
                                pool.sem_inc(slot_clear, 1)
                            elif j % 2 == 0:
                                early_weights_used(j)
                            k = g * GROUP + j
                            pool.indirect_dma_start(
                                u_row[j], None, u_table,
                                bass.IndirectOffsetOnAxis(ap=expert[b][:, k:k + 1], axis=0)).then_inc(u_landed[j], 16)
                        for j in range(GROUP):
                            k = g * GROUP + j
                            if isinstance(n, int) and n == 0 and g == 0:
                                if k % 2 == 0:
                                    early_weights_used(U_SLOTS + k)
                            else:
                                pool.wait_ge(v_used, TOPK * n + k - V_SLOTS + 1)
                                pool.sem_inc(slot_clear, 1)
                            pool.indirect_dma_start(
                                v_row[j], None, v_table,
                                bass.IndirectOffsetOnAxis(ap=expert[b][:, k:k + 1], axis=0)).then_inc(v_landed[j], 16)

            gather_pair(0)
            with pool.Fori(1, STEPS // 2) as i:
                gather_pair(i)

        @block.tensor
        def _(pe):
            taken = [0]

            def take(*name):
                n = FILL[name]
                assert n == taken[0], name
                taken[0] += 1
                before = [f for f in range(n) if fills[f][1] == fills[n][1]]
                if before:
                    pe.wait_ge(bank_read[fills[before[-1]][0]], nth(before[-1]))
                return banks[:, fills[n][1], :]

            def weights_of(*name):
                m = BLOCK[name]
                pe.wait_ge(w_landed[w_slot[m]], 16 * (before_in_slot(m)[1] + 1))
                return w_place[w_slot[m]]

            def to_features(bank, w, xt, tokens):
                for s in range(2):
                    for k in range(KT):
                        last = nc.tensor.matmul(bank[:, s * tokens:(s + 1) * tokens], w[:, k, s * P:(s + 1) * P], xt[:, k, :],
                                                start=(k == 0), stop=(k == KT - 1))
                last.then_inc(bank_done, 1)

            def to_tokens(bank, w, xt):
                for k in range(KT):
                    last = nc.tensor.matmul(bank, xt[:, k, :], w[:, k, :], start=(k == 0), stop=(k == KT - 1))
                return last

            def out_half(c, half):
                for q in range(2):
                    last = to_tokens(sums[:, 2 * c + half, q * COLS:(q + 1) * COLS], weights_of("out0", 2 * half + q),
                                     gatedT[:, :, c * P:(c + 1) * P])
                last.then_inc(out_done, 1)

            def transpose_norm(norm, c):
                pe.wait_ge(normed, normed_count(norm, c))
                for half in range(2):
                    bank = take("turn", norm, c, half)
                    for q in range(4):
                        k = 4 * half + q
                        last = nc.tensor.transpose(bank[:, q * P:(q + 1) * P], xn[:, c, k * P:(k + 1) * P], ident[:])
                    last.then_inc(bank_done, 1)

            def query(layer, c, hd):
                xt, n = (xT[:, :, :], T) if c == "both" else (xT[:, :, c * P:(c + 1) * P] if layer == 0 else kvT, P)
                to_features(take("query", layer, c, hd),
                            weights_of("query", layer + (layer and c), hd), xt, n)

            def score(layer, c, hd):
                wait_read(pe, "query", layer, c, hd)
                bank = take("score", layer, c, hd)
                for at in range(CH if c == "both" else 1):
                    for p in range(2):
                        last = nc.tensor.matmul(bank[:, (2 * at + p) * P:(2 * at + p + 1) * P],
                                                queryT[:, hd % 2, p, at * P:(at + 1) * P], subT[:, 2 * hd + p, :],
                                                start=True, stop=True)
                last.then_inc(bank_done, 1)

            def combine(n, b, g):
                if g == 0 and not (isinstance(n, int) and n < 2):
                    pe.wait_ge(head_added, n - 1)
                for k in range(g * GROUP, (g + 1) * GROUP):
                    pe.wait_ge(diag_ready, TOPK * n + k + 1)
                    pe.wait_ge(v_landed[k % V_SLOTS], 16 * (GROUPS * n + g + 1))
                    for half in range(2):
                        last = nc.tensor.matmul(sums[:, 2 * b + half, :], diag[:, k % GROUP, :],
                                                v_row[k % V_SLOTS][:, half * 512:(half + 1) * 512],
                                                start=(k == 0), stop=(k == TOPK - 1))
                    last.then_inc(v_used, 1)

            def combine_pair(i):
                for b in range(2):
                    for g in range(GROUPS):
                        combine(2 * i + b, b, g)

            def transpose_subkeys(layer):
                raw = weights_of("subkeys", layer).rearrange("p k n -> p (k n)")
                for n in range(2 * HEADS // 4):
                    bank = take("subkeys", layer, n)
                    for q in range(4):
                        r = 4 * n + q
                        last = nc.tensor.transpose(bank[:, q * P:(q + 1) * P], raw[:, r * KD:(r + 1) * KD], ident[:])
                    last.then_inc(bank_done, 1)

            def logits(c, j):
                for e in range(2):
                    bank, r = take("z", c, j, e), slice(e * DH, (e + 1) * DH)
                    for blk in range(1 - c, 2):
                        kc = c - 1 + blk
                        for q in range(2):
                            at, hp = 2 * blk + q, 2 * j + q
                            last = nc.tensor.matmul(bank[:, at * P:(at + 1) * P], keyT[r, hp, kc * P:(kc + 1) * P],
                                                    qryT[c][r, hp, :], start=(at == 2 - 2 * c), stop=True,
                                                    skip_group_check=True)
                    last.then_inc(bank_done, 1)

            def exponents(c, j):
                pe.wait_ge(soft_ready, NB * c + j + 1)
                for e in range(2):
                    bank, s = bank_of("z", c, j, e), notlog[:, e, :]
                    last = nc.tensor.matmul(bank[:, T:2 * T], later[:], s[:, T:2 * T], start=False, stop=True,
                                            skip_group_check=True)
                    if c:
                        nc.tensor.matmul(bank[:, 0:T], minus1[:], s[:, T:2 * T], start=False, stop=True,
                                         skip_group_check=True)
                        last = nc.tensor.matmul(bank[:, 0:T], later[:], s[:, 0:T], start=False, stop=True,
                                                skip_group_check=True)
                last.then_inc(expo_ready, 1)

            def heads_out(c, j):
                pe.wait_ge(weight_ready, NB * c + j + 1)
                bank = take("heads", c, j)
                for e in range(2):
                    for q in range(2):
                        for blk in range(1 - c, 2):
                            hd = 4 * j + 2 * q + e
                            last = nc.tensor.matmul(bank[e * DH:(e + 1) * DH, q * P:(q + 1) * P],
                                                    value[:, c - 1 + blk, hd * DH:(hd + 1) * DH],
                                                    soft[:, e, (2 * blk + q) * P:(2 * blk + q + 1) * P],
                                                    start=(q == 0 and blk == 1 - c), stop=(blk == 1),
                                                    skip_group_check=True)
                last.then_inc(bank_done, 1)

            def mixer_slot(c, t):
                if t == 0:
                    if c == 1:
                        for hd in (6, 7, 8):
                            if hd < HEADS:
                                query(1, 0, hd)
                            score(1, 0, hd - 1)
                    transpose_norm("kv", c)
                if t == 1:
                    wait_read(pe, "turn", "kv", c, 1)
                if t in (3, 5, 7, 9):
                    exponents(c, (t - 3) // 2)
                for name, j in PROJECTED.get(t, []):
                    if name == "z":
                        wait_read(pe, "qry", c, j)
                        logits(c, j)
                    elif name == "heads":
                        heads_out(c, j)
                    elif name == "val":
                        to_tokens(take(name, c, j)[:, 0:COLS], weights_of(name, c, j), kvT).then_inc(bank_done, 1)
                    else:
                        to_features(take(name, c, j), weights_of(name, c, j), kvT if name == "key" else mixT, P)
                if t == 7 and c == 0:
                    transpose_subkeys(1)
                if t == 10:
                    wait_read(pe, "heads", c, NB - 1)
                if t in (10, 11):
                    for q in (2 * (t - 10), 2 * (t - 10) + 1):
                        to_tokens(take("out", c, q)[:, 0:COLS], weights_of("out", q), headT[c]).then_inc(bank_done, 1)
                if t == 12:
                    transpose_norm("ffn1", c)
                    wait_read(pe, "turn", "ffn1", c, 1)
                    query(1, c, 0)
                for hd in {13: [1], 14: [2, 3], 15: [4, 5]}.get(t, []):
                    query(1, c, hd)
                    score(1, c, hd - 1)

            pe.wait_ge(consts, 10)
            pe.wait_ge(vec_loaded, 48)
            bank = take("vectors")
            nc.tensor.transpose(bank[:, 0:48], vec_rows[:, :], ident[0:48, 0:48]).then_inc(bank_done, 1)

            for c in range(CH):
                transpose_norm("mix0", c)
            wait_read(pe, "turn", "mix0", CH - 1, 1)
            def conv_group(c, j):
                xt, n = (xT, T) if c == "both" else (xT[:, :, c * P:(c + 1) * P], P)
                for part, _ in PARTS:
                    to_features(take("conv", c, j, part), weights_of("conv", j, part), xt, n)

            for j in range(NB):
                conv_group("both" if j < BOTH else 0, j)
            wait_read(pe, "conv", 0, NB - 1, 0)
            for half in range(2):
                out_half(0, half)
            transpose_subkeys(0)
            transpose_norm("ffn0", 0)
            wait_read(pe, "turn", "ffn0", 0, 1)
            query(0, 0, 0)
            score(0, 0, 0)
            for j in range(BOTH, NB):
                conv_group(1, j)
            query(0, 0, 1)
            score(0, 0, 1)

            for n in range(4):
                for g in range(GROUPS):
                    combine(n, n % 2, g)
                    t = GROUPS * n + g
                    if t == 0:
                        wait_read(pe, "conv", 1, NB - 1, 0)
                        for half in range(2):
                            out_half(1, half)
                    if t == 2:
                        transpose_norm("ffn0", 1)
                        wait_read(pe, "turn", "ffn0", 1, 1)
                    for c, hd in QUERIED.get(t, []):
                        query(0, c, hd)
                        score(0, c, hd)
            with pe.Fori(2, HEADS // 2) as i:
                combine_pair(i)
            for c in range(CH):
                for t in range(SLOTS):
                    n = HEADS * (1 + c) + t // GROUPS
                    combine(n, n % 2, t % GROUPS)
                    mixer_slot(c, t)
            first = (STEPS - HEADS) // 2
            combine(2 * first, 0, 0)
            for hd in (6, 7, 8):
                if hd < HEADS:
                    query(1, 1, hd)
                score(1, 1, hd - 1)
            combine(2 * first, 0, 1)
            for g in range(GROUPS):
                combine(2 * first + 1, 1, g)
            with pe.Fori(first + 1, STEPS // 2) as i:
                combine_pair(i)
            assert taken[0] == len(fills)

        @block.scalar
        def _(act):
            act.dma_start(gain[:], norm_ffn[0].partition_broadcast(P)).then_inc(gain_loaded, 16)

            steps = [0]

            def own(ins):
                ins.then_inc(act_step, 1)
                steps[0] += 1
                act.wait_ge(act_step, steps[0])

            read_last = [-1]

            def read(name, dst, view=lambda bank: bank, scale=1.0):
                n = FILL[name]
                assert fills[n][0] == "act" and n > read_last[0], name
                read_last[0] = n
                act.wait_ge(bank_done, n + 1)
                nc.scalar.activation(dst, view(banks[:, fills[n][1], :]), ACT.Copy, scale=scale).then_inc(bank_read["act"], 1)

            def by_tokens(bank):
                return bank.rearrange("p (k t) -> p k t", t=P)

            def norm_sums(norm, c):
                wait_input(act, norm, c)
                nc.scalar.activation(xn[:, c, :], h[:, c, :], ACT.Square, accum_out=stat[:, 0, c:c + 1]).then_inc(squares, 1)
                act.wait_ge(means, normed_count(norm, c))
                own(nc.scalar.activation(stat[:, 2, c:c + 1], stat[:, 1, c:c + 1], ACT.Ln))
                nc.scalar.activation(stat[:, 3, c:c + 1], stat[:, 2, c:c + 1], ACT.Exp, scale=-0.5).then_inc(estimates, 1)

            def turned_subkeys(layer):
                for j in range(2 * HEADS // 4):
                    read(("subkeys", layer, j), subT[:, 4 * j:4 * j + 4, :], by_tokens)

            def turned_norm(norm, c, dst):
                for half in range(2):
                    read(("turn", norm, c, half), dst[:, 4 * half:4 * half + 4, :], by_tokens)

            def queries(layer, c, hd):
                tokens = T if c == "both" else P
                if hd >= 2:
                    wait_filled(act, "score", layer, 1 if c == "both" and hd - 2 < FIRST else c, hd - 2)
                elif c == 1:
                    wait_filled(act, "score", layer, 0, max(o for o in range(HEADS if layer else FIRST) if o % 2 == hd))
                read(("query", layer, c, hd), queryT[:, hd % 2, :, 0:tokens],
                     lambda bank: bank[:, 0:2 * tokens].rearrange("p (s t) -> p s t", s=2))

            def scored(layer, c, hd):
                if c == "both":
                    read(("score", layer, c, hd), scores[:, hd:hd + HEADS + 1:HEADS, :],
                         lambda bank: bank.rearrange("p (c k) -> p c k", c=CH))
                else:
                    read(("score", layer, c, hd), scores[:, c * HEADS + hd, :], lambda bank: bank[:, 0:2 * KEYS])

            def gates(n, b):
                act.wait_ge(top_ready, n + 1)
                nc.scalar.activation(gate[b][:], top[b][:], ACT.Exp, bias=negmax[:, b:b + 1],
                                     accum_out=gate_sum[:, b:b + 1]).then_inc(gate_done, 1)

            def weigh(n, b, g):
                ks = slice(g * GROUP, (g + 1) * GROUP)
                act.wait_ge(dot_done, TOPK * n + GROUP * (g + 1))
                nc.scalar.activation(gelu[b][:, ks], dots[b][:, ks], ACT.Gelu).then_inc(gelu_done, 1)
                act.wait_ge(coef_ready, GROUPS * n + g + 1)
                for j in range(GROUP):
                    k = g * GROUP + j
                    if not (isinstance(n, int) and n == 0 and g == 0):
                        act.wait_ge(v_used, TOPK * n + k - GROUP + 1)
                    nc.scalar.activation(diag[:, j, :], ident[:], ACT.Copy, scale=coef[b][:, k:k + 1]).then_inc(diag_ready, 1)

            def weigh_pair(i, last=False):
                for b in range(2):
                    n = 2 * i + b
                    weigh(n, b, 0)
                    if not (last and b == 1):
                        gates(n + 1, 1 - b)
                    weigh(n, b, 1)

            def next_gain(norm, c, vector):
                act.wait_ge(normed, normed_count(norm, c))
                act.dma_start(gain[:], vector.partition_broadcast(P)).then_inc(gain_loaded, 16)

            def z_banks(c, j):
                return banks[:, 2:4, (1 - c) * T:]

            def logs(c, j):
                wait_filled(act, "z", c, j, 1)
                s = soft[:, :, (1 - c) * T:]
                nc.scalar.preload_act_table_set("natural_log_exp_and_others")
                own(nc.scalar.activation(s, z_banks(c, j), ACT.Abs))
                own(nc.scalar.activation(s, s, ACT.Exp, scale=-1.0))
                nc.scalar.activation(s, s, ACT.Ln, bias=1.0).then_inc(log_done, 1)

            def weights(c, j):
                wait_read(act, "z", c, j, 1)
                s = soft[:, :, (1 - c) * T:]
                nc.scalar.activation(s, s, ACT.Exp).then_inc(weight_ready, 1)

            def mixer_slot(c, t):
                if t in (0, 12):
                    nc.scalar.preload_act_table_set("natural_log_exp_and_others")
                    norm_sums("kv" if t == 0 else "ffn1", c)
                if t == 0 and c == 1:
                    for hd in (6, 7, 8):
                        if hd < HEADS:
                            queries(1, 0, hd)
                        scored(1, 0, hd - 1)
                for name, j in PROJECTED.get(t, []):
                    if name == "z":
                        logs(c, j)
                    elif name == "heads":
                        weights(c, j)
                        read(("heads", c, j), headT[c][:, 2 * j:2 * j + 2, :],
                             lambda bank: bank[:, 0:2 * P].rearrange("p (s t) -> p s t", s=2))
                    elif name == "val":
                        read((name, c, j), value[:, c, j * COLS:(j + 1) * COLS], lambda bank: bank[:, 0:COLS])
                    else:
                        dst = keyT[:, 2 * j:2 * j + 2, c * P:(c + 1) * P] if name == "key" else qryT[c][:, 2 * j:2 * j + 2, :]
                        read((name, c, j), dst, lambda bank: bank[:, 0:2 * P].rearrange("p (s t) -> p s t", s=2),
                             scale=1.0 if name == "key" else float(DH) ** -0.5)
                if t == 7 and c == 0:
                    turned_subkeys(1)
                if t == 12:
                    turned_norm("ffn1", c, kvT)
                    queries(1, c, 0)
                if t == 13 and c == 1:
                    next_gain("ffn1", 1, norm_final)
                for hd in {13: [1], 14: [2, 3], 15: [4, 5]}.get(t, []):
                    queries(1, c, hd)
                    scored(1, c, hd - 1)

            nc.scalar.preload_act_table_set("natural_log_exp_and_others")
            for c in range(CH):
                norm_sums("mix0", c)
            act.wait_ge(consts, 10)
            read(("vectors",), vecs[:, :], lambda bank: bank[:, 0:48])
            def conv_group(c, j):
                at = slice(0, T) if c == "both" else slice(c * P, (c + 1) * P)
                n = at.stop - at.start
                read(("conv", c, j, 2), conv_h[:, j % 2, :, at],
                     lambda bank: bank[:, 0:2 * n].rearrange("p (s t) -> p s t", s=2))

            for j in range(NB):
                if j >= 2:
                    wait_read(act, "conv", "both" if j - 2 < BOTH else 0, j - 2, 1)
                conv_group("both" if j < BOTH else 0, j)
            norm_sums("ffn0", 0)
            turned_subkeys(0)
            turned_norm("ffn0", 0, xT[:, :, 0:P])
            queries(0, 0, 0)
            scored(0, 0, 0)
            for j in range(BOTH, NB):
                if j >= BOTH + 2:
                    wait_read(act, "conv", 1, j - 2, 1)
                conv_group(1, j)
                if j == BOTH:
                    gates(0, 0)
            weigh(0, 0, 0)
            queries(0, 0, 1)
            scored(0, 0, 1)
            for n in range(4):
                for g in range(GROUPS):
                    t = GROUPS * n + g
                    if t > 0:
                        weigh(n, n % 2, g)
                    if g == 0:
                        gates(n + 1, 1 - n % 2)
                    if t == 1:
                        nc.scalar.preload_act_table_set("natural_log_exp_and_others")
                        norm_sums("ffn0", 1)
                    if t == 2:
                        turned_norm("ffn0", 1, xT[:, :, P:T])
                        next_gain("ffn0", CH - 1, norm_ffn[1])
                    for c, hd in QUERIED.get(t, []):
                        queries(0, c, hd)
                        scored(0, c, hd)
            with act.Fori(2, HEADS // 2) as i:
                weigh_pair(i)
            for c in range(CH):
                for t in range(SLOTS):
                    n = HEADS * (1 + c) + t // GROUPS
                    weigh(n, n % 2, t % GROUPS)
                    if t == SLOTS - 1 or (t % GROUPS == 0 and t < SLOTS - GROUPS):
                        gates(n + 1, 1 - n % 2)
                    mixer_slot(c, t)
            first = (STEPS - HEADS) // 2
            weigh(2 * first, 0, 0)
            gates(2 * first + 1, 1)
            nc.scalar.preload_act_table_set("natural_log_exp_and_others")
            norm_sums("final", 0)
            for hd in (6, 7, 8):
                if hd < HEADS:
                    queries(1, 1, hd)
                scored(1, 1, hd - 1)
            weigh(2 * first, 0, 1)
            weigh(2 * first + 1, 1, 0)
            gates(2 * first + 2, 0)
            weigh(2 * first + 1, 1, 1)
            with act.Fori(first + 1, STEPS // 2 - 1) as i:
                weigh_pair(i)
            weigh_pair(STEPS // 2 - 1, last=True)
            nc.scalar.preload_act_table_set("natural_log_exp_and_others")
            norm_sums("final", 1)

        @block.vector
        def _(dve):
            done = [0]

            def mark(ins):
                ins.then_inc(dve_step, 1)
                done[0] = done[0] + 1
                return done[0]

            def need(value):
                dve.wait_ge(dve_step, value)

            def need_apart(value):
                need(value)
                if not isinstance(value, int):
                    dve.sem_inc(search_clear, 1)

            def norm_stream(norm, c):
                mean, y, r, t = (stat[:, q, c:c + 1] for q in (1, 3, 4, 5))
                dve.wait_ge(squares, normed_count(norm, c))
                nc.vector.tensor_scalar(mean, stat[:, 0, c:c + 1], 1.0 / D, EPS, ALU.mult, ALU.add).then_inc(means, 1)
                dve.wait_ge(estimates, normed_count(norm, c))
                need(mark(nc.vector.tensor_tensor(t, y, y, ALU.mult)))
                need(mark(nc.vector.tensor_tensor(t, t, mean, ALU.mult)))
                need(mark(nc.vector.tensor_scalar(t, t, -0.5, 1.5, ALU.mult, ALU.add)))
                need(mark(nc.vector.tensor_tensor(r, y, t, ALU.mult)))
                if norm in ("mix0", "kv"):
                    nc.vector.tensor_scalar(xn[:, c, :], h[:, c, :], r, None, ALU.mult).then_inc(normed, 1)
                else:
                    dve.wait_ge(gain_loaded, 16 * (1 + ["ffn0", "ffn1", "final"].index(norm)))
                    nc.vector.scalar_tensor_tensor(out=xn[:, c, :], in0=h[:, c, :], scalar=r, in1=gain[:],
                                                   op0=ALU.mult, op1=ALU.mult).then_inc(normed, 1)

            def turned_norm(norm, c, outs):
                for half in range(2):
                    wait_filled(dve, "turn", norm, c, half)
                    for t, (dst, col) in enumerate(outs):
                        g = vecs[:, col + 4 * half:col + 4 * half + 4].unsqueeze(2).to_broadcast([P, 4, P])
                        ins = nc.vector.tensor_tensor(dst[:, 4 * half:4 * half + 4, :],
                                                      bank_of("turn", norm, c, half).rearrange("p (k t) -> p k t", t=P), g, ALU.mult)
                    ins.then_inc(bank_read["dve"], 1)

            def add_mixer(c):
                for half in range(2):
                    dve.wait_ge(out_done, 2 * c + half + 1)
                    at = h[:, c, half * 512:(half + 1) * 512]
                    nc.vector.tensor_tensor(at, sums[:, 2 * c + half, :], at, ALU.add).then_inc(out_added, 1)

            def top16(values, indices, src, scratch, start):
                need_apart(start)
                a = mark(nc.vector.max(values[:, 0:8], src))
                need_apart(a)
                r = mark(nc.vector.match_replace(scratch, values[:, 0:8], src, FOUND))
                mark(nc.vector.max_index(indices[:, 0:8], values[:, 0:8], src))
                need_apart(r)
                b = mark(nc.vector.max(values[:, 8:16], scratch))
                need_apart(b)
                return mark(nc.vector.max_index(indices[:, 8:16], values[:, 8:16], scratch))

            def find_experts(n, at, b, layer):
                s = mark(nc.vector.tensor_copy(srch, scores[:, bass.ds(at, 1), :].rearrange("p a k -> p (a k)")))
                for p in range(2):
                    e = top16(side_v[:, p, :], side_i[:, p, :], srch[:, p * KEYS:(p + 1) * KEYS],
                              srch2[:, p * KEYS:(p + 1) * KEYS], s)
                need(e)
                c = mark(nc.vector.tensor_tensor(cand.rearrange("p (a b) -> p a b", b=TOPK),
                                                 side_v[:, 0, :].unsqueeze(2).to_broadcast([P, TOPK, TOPK]),
                                                 side_v[:, 1, :].unsqueeze(1).to_broadcast([P, TOPK, TOPK]), ALU.add))
                e = top16(top[b][:], cand_i[:], cand, cand2, c)
                need(e)
                nc.vector.tensor_scalar(negmax[:, b:b + 1], top[b][:, 0:1], -1.0, None, ALU.mult).then_inc(top_ready, 1)
                mark(nc.vector.tensor_scalar(digit[:, 0, :], cand_i[:], 4, None, ALU.logical_shift_right))
                d = mark(nc.vector.tensor_scalar(digit[:, 1, :], cand_i[:], TOPK - 1, None, ALU.bitwise_and))
                need(d)
                d = mark(nc.vector.tensor_tensor(pick.rearrange("p a k j -> p (a k) j"),
                                                 digit[:].rearrange("p a k -> p (a k)").unsqueeze(2).to_broadcast([P, 2 * TOPK, TOPK]),
                                                 iota[:].unsqueeze(1).to_broadcast([P, 2 * TOPK, TOPK]), ALU.is_equal))
                need(d)
                d = mark(nc.vector.tensor_tensor(pick, pick,
                                                 side_i[:].unsqueeze(2).to_broadcast([P, 2, TOPK, TOPK]), ALU.mult))
                need(d)
                d = mark(nc.vector.tensor_reduce(picked[:].rearrange("p a k -> p (a k)"),
                                                 pick.rearrange("p a k j -> p (a k) j"), AX_X, ALU.add))
                need(d)
                d = mark(nc.vector.scalar_tensor_tensor(out=expert_f[:], in0=picked[:, 0, :], scalar=float(KEYS),
                                                        in1=picked[:, 1, :], op0=ALU.mult, op1=ALU.add))
                need(d)
                nc.vector.tensor_scalar(expert[b][:], expert_f[:], float(layer * EXPERTS), None, ALU.add).then_inc(expert_ready, 1)

            def dot_group(n, chunk, b, g):
                for j in range(GROUP):
                    k = g * GROUP + j
                    dve.wait_ge(u_landed[j], 16 * (GROUPS * n + g + 1))
                    nc.vector.scalar_tensor_tensor(out=u_row[j], in0=u_row[j], scalar=1.0,
                                                   in1=xn[:, bass.ds(chunk, 1), :].rearrange("p c d -> p (c d)"),
                                                   op0=ALU.mult, op1=ALU.mult,
                                                   accum_out=dots[b][:, k:k + 1]).then_inc(dot_done, 1)

            def add_head(n, chunk, b):
                dve.wait_ge(v_used, TOPK * (n + 1))
                at = h[:, bass.ds(chunk, 1), :].rearrange("p c d -> p (c d)")
                nc.vector.tensor_tensor(at, sums[:, 2 * b:2 * b + 2, :].rearrange("p a d -> p (a d)"), at,
                                        ALU.add).then_inc(head_added, 1)

            def coefficients(n, b, g):
                dve.wait_ge(gelu_done, GROUPS * n + g + 1)
                if g == 0:
                    dve.wait_ge(gate_done, n + 1)
                    need(mark(nc.vector.reciprocal(gate_inv[:, b:b + 1], gate_sum[:, b:b + 1])))
                ks = slice(g * GROUP, (g + 1) * GROUP)
                nc.vector.scalar_tensor_tensor(out=coef[b][:, ks], in0=gelu[b][:, ks], scalar=gate_inv[:, b:b + 1],
                                               in1=gate[b][:, ks], op0=ALU.mult, op1=ALU.mult).then_inc(coef_ready, 1)

            def step(n, b, chunk, before, at, layer, look=True, scored=None):
                dot_group(n, chunk, b, 0)
                if not (isinstance(n, int) and n == 0):
                    add_head(n - 1, before, 1 - b)
                coefficients(n, b, 0)
                if scored:
                    wait_read(dve, *scored)
                if look:
                    find_experts(n + 1, at, 1 - b, layer)

            def second_group(n, b, chunk):
                dot_group(n, chunk, b, 1)
                coefficients(n, b, 1)

            def expert_pair(i, chunk, layer, last=False):
                scored = ("score", 0, "both", HEADS - 1) if layer == 0 else ("score", 1, chunk, HEADS - 1)
                for b in range(2):
                    n = 2 * i + b
                    step(n, b, chunk, chunk, n + 1 - NH * layer, layer, look=not (last and b == 1), scored=scored)
                    second_group(n, b, chunk)

            def looped_pairs(first, end, per, chunk, layer):
                start = done[0]
                with dve.Fori(first, end) as i:
                    done[0] = start - per * first + per * i
                    expert_pair(i, chunk, layer)
                done[0] = start + per * (end - first)

            def z_banks(c, j):
                return banks[:, 2:4, (1 - c) * T:]

            def softplus(c, j):
                dve.wait_ge(log_done, NB * c + j + 1)
                s = notlog[:, :, (1 - c) * T:]
                need(mark(nc.vector.scalar_tensor_tensor(out=s, in0=z_banks(c, j), scalar=0.0, in1=soft[:, :, (1 - c) * T:],
                                                         op0=ALU.max, op1=ALU.add)))
                d = notlog[:, :, T:].rearrange("p e (q t) -> p e q t", t=P)
                nc.vector.tensor_tensor(d, d, keep[:].unsqueeze(1).unsqueeze(1).to_broadcast([P, 2, 2, P]),
                                        ALU.mult).then_inc(soft_ready, 1)

            def exponent(c, j):
                dve.wait_ge(expo_ready, NB * c + j + 1)
                if c:
                    nc.vector.tensor_scalar(soft[:, :, 0:T], banks[:, 2:4, 0:T], 0.0, None, ALU.min)
                for e in range(2):
                    nc.vector.scalar_tensor_tensor(out=soft[:, e, T:].rearrange("p (q t) -> p q t", t=P),
                                                   in0=bank_of("z", c, j, e)[:, T:].rearrange("p (q t) -> p q t", t=P),
                                                   scalar=0.0, in1=hide[:].unsqueeze(1).to_broadcast([P, 2, P]),
                                                   op0=ALU.min, op1=ALU.add).then_inc(bank_read["dve"], 1)

            def mixer_slot(c, t):
                if t == 0:
                    norm_stream("kv", c)
                if t == 1:
                    turned_norm("kv", c, [(kvT, 2 * KT), (mixT, KT)])
                if t in (3, 5, 7, 9):
                    softplus(c, (t - 3) // 2)
                if t in (4, 6, 8, 10):
                    exponent(c, (t - 4) // 2)
                if t == 12:
                    for q in range(NB):
                        wait_filled(dve, "out", c, q)
                        at = h[:, c, q * COLS:(q + 1) * COLS]
                        nc.vector.tensor_tensor(at, bank_of("out", c, q)[:, 0:COLS], at, ALU.add).then_inc(bank_read["dve"], 1)
                    norm_stream("ffn1", c)

            for b in range(2):
                mark(nc.vector.memset(conv_u[:, b, :, 0:TAPS - 1], 0.0))
            for c in range(CH):
                norm_stream("mix0", c)
            wait_read(dve, "vectors")
            for c in range(CH):
                turned_norm("mix0", c, [(xT[:, :, c * P:(c + 1) * P], 0)])
            def conv_group(c, j):
                at = slice(0, T) if c == "both" else slice(c * P, (c + 1) * P)
                n = at.stop - at.start
                u, y = conv_u[:, j % 2], conv_y[:, j % 2, :, at]
                c_bank, b_bank = (bank_of("conv", c, j, part)[:, 0:2 * n].rearrange("p (s t) -> p s t", s=2) for part in (1, 0))
                wait_read(dve, "conv", c, j, 2)
                wait_filled(dve, "conv", c, j, 1)
                nc.vector.tensor_tensor(u[:, :, TAPS - 1 + at.start:TAPS - 1 + at.stop], c_bank, conv_h[:, j % 2, :, at],
                                        ALU.mult).then_inc(bank_read["dve"], 1)
                wait_read(dve, "conv", c, j, 1)
                if c == 0:
                    mark(nc.vector.tensor_copy(conv_halo[:, j], u[:, :, P:P + TAPS - 1]))
                elif c == 1:
                    need(mark(nc.vector.tensor_copy(u[:, :, P:P + TAPS - 1], conv_halo[:, j])))
                written = [0, 0]
                for i in range(TAPS):
                    for s in range(2):
                        src = u[:, s, at.start + i:at.stop + i]
                        tap = vecs[:, (3 + i) * KT + 2 * j + s:(3 + i) * KT + 2 * j + s + 1]
                        if i == 0:
                            written[s] = mark(nc.vector.tensor_scalar(y[:, s, :], src, tap, None, ALU.mult))
                        else:
                            need(written[s])
                            written[s] = mark(nc.vector.scalar_tensor_tensor(out=y[:, s, :], in0=src, scalar=tap, in1=y[:, s, :],
                                                                             op0=ALU.mult, op1=ALU.add))
                need(written[1])
                wait_filled(dve, "conv", c, j, 0)
                nc.vector.tensor_tensor(gatedT[:, 2 * j:2 * j + 2, at], b_bank, y, ALU.mult).then_inc(bank_read["dve"], 1)

            for j in range(NB):
                conv_group("both" if j < BOTH else 0, j)
            add_mixer(0)
            norm_stream("ffn0", 0)
            wait_read(dve, "score", 0, 0, 0)
            find_experts(0, 0, 0, 0)

            for j in range(BOTH, NB - 1):
                conv_group(1, j)
            dot_group(0, 0, 0, 0)
            conv_group(1, NB - 1)
            coefficients(0, 0, 0)
            wait_read(dve, "score", 0, 0, 1)
            find_experts(1, 1, 1, 0)
            second_group(0, 0, 0)
            add_mixer(1)
            norm_stream("ffn0", 1)
            for n in range(1, 4):
                before = done[0]
                step(n, n % 2, 0, 0, n + 1, 0, scored=("score", 0, "both" if n + 1 >= FIRST else 0, n + 1))
                second_group(n, n % 2, 0)
                per = 2 * (done[0] - before)
            looped_pairs(2, HEADS // 2, per, 0, 0)

            for c in range(CH):
                chunk = 1 - c
                for t in range(SLOTS):
                    hd = t // GROUPS
                    n = HEADS * (1 + c) + hd
                    b = n % 2
                    if t % GROUPS == 0:
                        look = hd + 1 < HEADS
                        step(n, b, chunk, chunk if hd else c, n + 1 - NH * c, c, look,
                             ("score", 1, 0, hd + 1) if c == 1 and look else None)
                    else:
                        second_group(n, b, chunk)
                    if t == SLOTS - 1:
                        wait_read(dve, "score", 1, c, 0)
                        find_experts(n + 1, n + 1 - NH, 1 - b, 1)
                    mixer_slot(c, t)

            first = (STEPS - HEADS) // 2
            step(2 * first, 0, 1, 0, HEADS + 1, 1, scored=("score", 1, 1, 1))
            norm_stream("final", 0)
            second_group(2 * first, 0, 1)
            step(2 * first + 1, 1, 1, 1, HEADS + 2, 1, scored=("score", 1, 1, 2))
            second_group(2 * first + 1, 1, 1)
            looped_pairs(first + 1, STEPS // 2 - 1, per, 1, 1)
            expert_pair(STEPS // 2 - 1, 1, 1, last=True)
            add_head(STEPS - 1, 1, 1)
            norm_stream("final", 1)


_INS = ["x", "norm_mix", "norm_ffn", "conv_w_in", "conv_kernel", "conv_w_out", "norm_kv", "w_kv", "attn_w_q",
        "attn_w_o", "peer_w_query", "peer_subkeys", "peer_u", "peer_v", "norm_final"]


def kernel(**inputs):
    import numpy as _np
    import concourse.bacc as _bacc
    from concourse import mybir as _mybir
    from concourse.bass_utils import run_bass_kernel_spmd as _run

    nc = _bacc.Bacc("TRN2", target_bir_lowering=False, num_devices=1)
    arrays, args = {}, []
    for name in _INS:
        a = _np.ascontiguousarray(inputs[name])
        arrays[f"in_{name}"] = a
        args.append(nc.dram_tensor(f"in_{name}", a.shape, _mybir.dt.from_np(a.dtype), kind="ExternalInput").ap())
    shape = inputs["x"].shape
    args.append(nc.dram_tensor("out_stream", shape, _mybir.dt.float32, kind="ExternalOutput").ap())
    trunk(nc, *args)
    r = _run(nc, [arrays], core_ids=[0])
    return r.results[0]["out_stream"]
```
